# Optimizing a Trainium2 kernel written in Bass

```python
import math
import jax
import jax.numpy as jnp
from jax import lax
import numpy as np

D_MODEL = 1024
BATCH = 1
SEQ = 256
DEPTH = 2

CTX_LEN = 256
GRID_W = 64
N_MOD = 6
CONV_DIM = 512
CONV_K = 31
MLA_HEADS = 8
Q_LORA = 384
KV_LORA = 256
QK_NOPE = 64
QK_ROPE = 32
V_HEAD = 64
QK_HEAD = QK_NOPE + QK_ROPE
AXIS_PAIRS = QK_ROPE // 4
ROPE_THETA = 10000.0
SOFTMAX_SCALE = 1.0 / math.sqrt(QK_HEAD)
Q_BLOCK = 128
GMLP_DIM = 512
GMLP_GROUPS = 8
GMLP_GROUP_DIM = GMLP_DIM // GMLP_GROUPS
CHUNK = 128
N_BRANCH = 3
COL_Q = 2 * CONV_DIM
COL_KV = COL_Q + Q_LORA
COL_KR = COL_KV + KV_LORA
COL_GM = COL_KR + QK_ROPE
COL_GATE = COL_GM + 2 * GMLP_DIM
IN_DIM = COL_GATE + N_BRANCH * D_MODEL
D_FF = 2816
N_EXPERTS = 8
TOP_K = 2
D_FF_EXPERT = 3584
MOE_BLOCK = 128
N_DENSE_LAYERS = (DEPTH + 1) // 2
N_MOE_LAYERS = DEPTH // 2
RMS_EPS = 1e-6
LN_EPS = 1e-5

kernel_name = "hybrid_conv_mla_gmlp_moe_dit"

def rms_norm(x, g):
    xf = x.astype(jnp.float32)
    y = xf * lax.rsqrt(jnp.mean(xf * xf, axis=-1, keepdims=True) + RMS_EPS)
    return (y * g.astype(jnp.float32)).astype(x.dtype)

def layer_norm(x, g, b):
    xf = x.astype(jnp.float32)
    xc = xf - jnp.mean(xf, axis=-1, keepdims=True)
    var = jnp.mean(xc * xc, axis=-1, keepdims=True)
    y = xc * lax.rsqrt(var + LN_EPS) * g.astype(jnp.float32) + b.astype(jnp.float32)
    return y.astype(x.dtype)

def modulate(h, shift, scale):
    return h * (1 + scale) + shift

def axial_angles(rows):
    row = jnp.repeat(jnp.arange(rows, dtype=jnp.float32), GRID_W)
    col = jnp.tile(jnp.arange(GRID_W, dtype=jnp.float32), rows)
    inv_freq = ROPE_THETA ** (-jnp.arange(AXIS_PAIRS, dtype=jnp.float32) / AXIS_PAIRS)
    return row[:, None] * inv_freq, col[:, None] * inv_freq

def rotate_pairs(x, ang):
    x1, x2 = jnp.split(x, 2, axis=-1)
    cos = jnp.cos(ang).astype(x.dtype)
    sin = jnp.sin(ang).astype(x.dtype)
    return jnp.concatenate([x1 * cos - x2 * sin, x1 * sin + x2 * cos], axis=-1)

def axial_rope(x, ang_row, ang_col):
    xr, xc = jnp.split(x, 2, axis=-1)
    return jnp.concatenate([rotate_pairs(xr, ang_row[None, :, None, :]),
                            rotate_pairs(xc, ang_col[None, :, None, :])], axis=-1)

def mla_query(c_q, q_norm_g, w_uq, angles):
    b, n, _ = c_q.shape
    q = (rms_norm(c_q, q_norm_g) @ w_uq).reshape(b, n, MLA_HEADS, QK_HEAD)
    q_nope, q_rope = q[..., :QK_NOPE], q[..., QK_NOPE:]
    if angles is not None:
        q_rope = axial_rope(q_rope, angles[0], angles[1])
    return jnp.concatenate([q_nope, q_rope], axis=-1)

def mla_key_value(c_kv, k_rope, kv_norm_g, w_ukv, angles):
    b, n, _ = c_kv.shape
    kv = (rms_norm(c_kv, kv_norm_g) @ w_ukv).reshape(b, n, MLA_HEADS, QK_NOPE + V_HEAD)
    k_nope, v = kv[..., :QK_NOPE], kv[..., QK_NOPE:]
    k_rope = k_rope[:, :, None, :]
    if angles is not None:
        k_rope = axial_rope(k_rope, angles[0], angles[1])
    k = jnp.concatenate([k_nope, jnp.broadcast_to(k_rope, (b, n, MLA_HEADS, QK_ROPE))], axis=-1)
    return k, v

def attend(q, k, v):
    s = jnp.einsum('bqhd,bkhd->bhqk', q, k).astype(jnp.float32) * SOFTMAX_SCALE
    p = jax.nn.softmax(s, axis=-1).astype(v.dtype)
    return jnp.einsum('bhqk,bkhd->bqhd', p, v)

def latent_attention(q, k_all, v_all):
    b, n, h, dk = q.shape
    q_blocks = q.reshape(b, n // Q_BLOCK, Q_BLOCK, h, dk).transpose(1, 0, 2, 3, 4)
    o = lax.map(lambda qb: attend(qb, k_all, v_all), q_blocks)
    return o.transpose(1, 0, 2, 3, 4).reshape(b, n, h * V_HEAD)

def conformer_conv(z, dw, db, ln_g, ln_b, w_proj):
    a, gate = jnp.split(z, 2, axis=-1)
    u = a * jax.nn.sigmoid(gate)
    u = lax.conv_general_dilated(u, dw[:, None, :].astype(u.dtype), window_strides=(1,),
                                 padding=[(CONV_K // 2, CONV_K // 2)],
                                 dimension_numbers=('NWC', 'WIO', 'NWC'),
                                 feature_group_count=CONV_DIM) + db
    u = jax.nn.silu(layer_norm(u, ln_g, ln_b))
    return u @ w_proj

def chunk_gmlp(z, ln_g, ln_b, w_s, b_s, w_proj):
    b, n, _ = z.shape
    u, v = jnp.split(jax.nn.gelu(z), 2, axis=-1)
    v = layer_norm(v, ln_g, ln_b).reshape(b, n // CHUNK, CHUNK, GMLP_GROUPS, GMLP_GROUP_DIM)
    s = jnp.einsum('gpq,bcqgd->bcpgd', w_s, v) + b_s.T[:, :, None]
    return (u * s.reshape(b, n, GMLP_DIM)) @ w_proj

def split_columns(z):
    return jnp.split(z, [COL_Q, COL_KV, COL_KR, COL_GM, COL_GATE], axis=-1)

def mixer_output(zs, attn_heads, b_gate, conv_dw, conv_db, conv_ln_g, conv_ln_b, w_conv_out,
                 w_attn_out, gmlp_ln_g, gmlp_ln_b, w_spatial, b_spatial, w_gmlp_out, w_out):
    z_conv, z_gmlp, z_gate = zs[0], zs[4], zs[5]
    br_conv = conformer_conv(z_conv, conv_dw, conv_db, conv_ln_g, conv_ln_b, w_conv_out)
    br_attn = attn_heads @ w_attn_out
    br_gmlp = chunk_gmlp(z_gmlp, gmlp_ln_g, gmlp_ln_b, w_spatial, b_spatial, w_gmlp_out)
    gates = jax.nn.sigmoid((z_gate + b_gate).astype(jnp.float32)).astype(z_gate.dtype)
    g_conv, g_attn, g_gmlp = jnp.split(gates, N_BRANCH, axis=-1)
    return (g_conv * br_conv + g_attn * br_attn + g_gmlp * br_gmlp) @ w_out

def token_mixer(a_lat, a_ctx, angles, need_ctx, w_in, b_gate, conv_dw, conv_db, conv_ln_g,
                conv_ln_b, w_conv_out, q_norm_g, w_uq, kv_norm_g, w_ukv, w_attn_out, gmlp_ln_g,
                gmlp_ln_b, w_spatial, b_spatial, w_gmlp_out, w_out):
    zl = split_columns(a_lat @ w_in)
    zc = split_columns(a_ctx @ w_in)
    k_ctx, v_ctx = mla_key_value(zc[2], zc[3], kv_norm_g, w_ukv, None)
    k_lat, v_lat = mla_key_value(zl[2], zl[3], kv_norm_g, w_ukv, angles)
    q_lat = mla_query(zl[1], q_norm_g, w_uq, angles)
    o_lat = latent_attention(q_lat, jnp.concatenate([k_lat, k_ctx], axis=1),
                             jnp.concatenate([v_lat, v_ctx], axis=1))
    y_lat = mixer_output(zl, o_lat, b_gate, conv_dw, conv_db, conv_ln_g, conv_ln_b, w_conv_out,
                         w_attn_out, gmlp_ln_g, gmlp_ln_b, w_spatial, b_spatial, w_gmlp_out, w_out)
    y_ctx = None
    if need_ctx:
        b, n_ctx = a_ctx.shape[0], a_ctx.shape[1]
        q_ctx = mla_query(zc[1], q_norm_g, w_uq, None)
        o_ctx = attend(q_ctx, k_ctx, v_ctx).reshape(b, n_ctx, MLA_HEADS * V_HEAD)
        y_ctx = mixer_output(zc, o_ctx, b_gate, conv_dw, conv_db, conv_ln_g, conv_ln_b,
                             w_conv_out, w_attn_out, gmlp_ln_g, gmlp_ln_b, w_spatial, b_spatial,
                             w_gmlp_out, w_out)
    return y_lat, y_ctx

def swiglu(h, w13, w2):
    a, g = jnp.split(h @ w13, 2, axis=-1)
    return (jax.nn.silu(a) * g) @ w2

def moe_swiglu(h, w_router, w13, w2):
    n_tok, d = h.shape
    n_assign = n_tok * TOP_K
    logits = (h @ w_router).astype(jnp.float32)
    top_logit, top_expert = lax.top_k(logits, TOP_K)
    top_w = jax.nn.softmax(top_logit, axis=-1).astype(h.dtype)
    expert = top_expert.reshape(-1)
    token = jnp.repeat(jnp.arange(n_tok), TOP_K)
    order = jnp.argsort(expert)
    expert_s, token_s, w_s = expert[order], token[order], top_w.reshape(-1)[order]
    counts = jnp.bincount(expert, length=N_EXPERTS)
    starts = jnp.cumsum(counts) - counts
    padded = (counts + MOE_BLOCK - 1) // MOE_BLOCK * MOE_BLOCK
    padded_end = jnp.cumsum(padded)
    dest = (padded_end - padded)[expert_s] + jnp.arange(n_assign) - starts[expert_s]
    n_rows = -(-n_assign // MOE_BLOCK) * MOE_BLOCK + N_EXPERTS * MOE_BLOCK
    n_blocks = n_rows // MOE_BLOCK
    rows = jnp.zeros((n_rows, d), h.dtype).at[dest].set(h[token_s])
    block_expert = jnp.minimum(
        jnp.searchsorted(padded_end, jnp.arange(n_blocks) * MOE_BLOCK, side='right'), N_EXPERTS - 1)

    def expert_block(args):
        xb, e = args
        a, g = jnp.split(xb @ w13[e], 2, axis=-1)
        return (jax.nn.silu(a) * g) @ w2[e]

    out = lax.map(expert_block, (rows.reshape(n_blocks, MOE_BLOCK, d), block_expert))
    y = out.reshape(n_rows, d)[dest] * w_s[:, None]
    return jnp.zeros_like(h).at[token_s].add(y)

def setup_inputs(seed: int = 0) -> dict:
    key = jax.random.key(seed)
    ks = jax.random.split(key, 32)
    L, D = DEPTH, D_MODEL

    def nrm(k, shape, scale):
        return jax.random.normal(k, shape, jnp.float32) * scale

    return {
        'x': nrm(ks[0], (BATCH, SEQ, D), 1.0),
        'c': nrm(ks[1], (BATCH, D), 1.0),
        'ctx': nrm(ks[2], (BATCH, CTX_LEN, D), 1.0),
        'c_ctx': nrm(ks[3], (D,), 1.0),
        'w_mod': nrm(ks[4], (L, D, N_MOD * D), D ** -0.5),
        'b_mod': nrm(ks[5], (L, N_MOD * D), 0.02),
        'norm_g': 1.0 + nrm(ks[6], (L, 4, D), 0.02),
        'w_in': nrm(ks[7], (L, D, IN_DIM), D ** -0.5),
        'b_gate': nrm(ks[8], (L, N_BRANCH * D), 0.02),
        'conv_dw': nrm(ks[9], (L, CONV_K, CONV_DIM), CONV_K ** -0.5),
        'conv_db': nrm(ks[10], (L, CONV_DIM), 0.02),
        'conv_ln_g': 1.0 + nrm(ks[11], (L, CONV_DIM), 0.02),
        'conv_ln_b': nrm(ks[12], (L, CONV_DIM), 0.02),
        'w_conv_out': nrm(ks[13], (L, CONV_DIM, D), CONV_DIM ** -0.5),
        'q_norm_g': 1.0 + nrm(ks[14], (L, Q_LORA), 0.02),
        'w_uq': nrm(ks[15], (L, Q_LORA, MLA_HEADS * QK_HEAD), Q_LORA ** -0.5),
        'kv_norm_g': 1.0 + nrm(ks[16], (L, KV_LORA), 0.02),
        'w_ukv': nrm(ks[17], (L, KV_LORA, MLA_HEADS * (QK_NOPE + V_HEAD)), KV_LORA ** -0.5),
        'w_attn_out': nrm(ks[18], (L, MLA_HEADS * V_HEAD, D), (MLA_HEADS * V_HEAD) ** -0.5),
        'gmlp_ln_g': 1.0 + nrm(ks[19], (L, GMLP_DIM), 0.02),
        'gmlp_ln_b': nrm(ks[20], (L, GMLP_DIM), 0.02),
        'w_spatial': nrm(ks[21], (L, GMLP_GROUPS, CHUNK, CHUNK), CHUNK ** -0.5),
        'b_spatial': 1.0 + nrm(ks[22], (L, GMLP_GROUPS, CHUNK), 0.02),
        'w_gmlp_out': nrm(ks[23], (L, GMLP_DIM, D), GMLP_DIM ** -0.5),
        'w_out': nrm(ks[24], (L, D, D), D ** -0.5),
        'ffn_w13': nrm(ks[25], (N_DENSE_LAYERS, D, 2 * D_FF), D ** -0.5),
        'ffn_w2': nrm(ks[26], (N_DENSE_LAYERS, D_FF, D), D_FF ** -0.5),
        'router_w': nrm(ks[27], (N_MOE_LAYERS, D, N_EXPERTS), D ** -0.5),
        'moe_w13': nrm(ks[28], (N_MOE_LAYERS, N_EXPERTS, D, 2 * D_FF_EXPERT), D ** -0.5),
        'moe_w2': nrm(ks[29], (N_MOE_LAYERS, N_EXPERTS, D_FF_EXPERT, D), D_FF_EXPERT ** -0.5),
    }

def reference(x, c, ctx, c_ctx, w_mod, b_mod, norm_g, w_in, b_gate, conv_dw, conv_db, conv_ln_g,
              conv_ln_b, w_conv_out, q_norm_g, w_uq, kv_norm_g, w_ukv, w_attn_out, gmlp_ln_g,
              gmlp_ln_b, w_spatial, b_spatial, w_gmlp_out, w_out, ffn_w13, ffn_w2, router_w,
              moe_w13, moe_w2):
    bsz, n_lat, d = x.shape
    rows = n_lat // GRID_W
    angles = axial_angles(rows)
    h_lat, h_ctx = x, ctx
    for layer in range(DEPTH):
        need_ctx = layer < DEPTH - 1
        mod_lat = (jax.nn.silu(c) @ w_mod[layer] + b_mod[layer])[:, None, :]
        mod_ctx = jax.nn.silu(c_ctx) @ w_mod[layer] + b_mod[layer]
        sh_t, sc_t, gt_t, sh_f, sc_f, gt_f = jnp.split(mod_lat, N_MOD, axis=-1)
        csh_t, csc_t, cgt_t, csh_f, csc_f, cgt_f = jnp.split(mod_ctx, N_MOD, axis=-1)
        g_pre_t, g_post_t = norm_g[layer, 0], norm_g[layer, 1]
        g_pre_f, g_post_f = norm_g[layer, 2], norm_g[layer, 3]

        a_lat = modulate(rms_norm(h_lat, g_pre_t), sh_t, sc_t)
        a_ctx = modulate(rms_norm(h_ctx, g_pre_t), csh_t, csc_t)
        y_lat, y_ctx = token_mixer(
            a_lat, a_ctx, angles, need_ctx, w_in[layer], b_gate[layer], conv_dw[layer],
            conv_db[layer], conv_ln_g[layer], conv_ln_b[layer], w_conv_out[layer],
            q_norm_g[layer], w_uq[layer], kv_norm_g[layer], w_ukv[layer], w_attn_out[layer],
            gmlp_ln_g[layer], gmlp_ln_b[layer], w_spatial[layer], b_spatial[layer],
            w_gmlp_out[layer], w_out[layer])
        h_lat = h_lat + gt_t * rms_norm(y_lat, g_post_t)
        if need_ctx:
            h_ctx = h_ctx + cgt_t * rms_norm(y_ctx, g_post_t)

        f_lat_in = modulate(rms_norm(h_lat, g_pre_f), sh_f, sc_f)
        if need_ctx:
            f_ctx_in = modulate(rms_norm(h_ctx, g_pre_f), csh_f, csc_f)
            tokens = jnp.concatenate([f_lat_in.reshape(-1, d), f_ctx_in.reshape(-1, d)], axis=0)
        else:
            tokens = f_lat_in.reshape(-1, d)
        idx = layer // 2
        if layer % 2 == 0:
            f = swiglu(tokens, ffn_w13[idx], ffn_w2[idx])
        else:
            f = moe_swiglu(tokens, router_w[idx], moe_w13[idx], moe_w2[idx])
        f_lat = f[: bsz * n_lat].reshape(bsz, n_lat, d)
        h_lat = h_lat + gt_f * rms_norm(f_lat, g_post_f)
        if need_ctx:
            f_ctx = f[bsz * n_lat:].reshape(bsz, -1, d)
            h_ctx = h_ctx + cgt_f * rms_norm(f_ctx, g_post_f)
    return h_lat


_drawn_inputs = setup_inputs


def setup_inputs(seed=0):
    import zlib

    import numpy as np

    out = dict(_drawn_inputs(seed))
    spreads = {}
    factors = {'conv_ln_g': 7.989,
     'conv_ln_b': 9.087,
     'q_norm_g': 8.0,
     'kv_norm_g': 8.0,
     'gmlp_ln_g': 3.474,
     'gmlp_ln_b': 4.061,
     'b_spatial': 3.888}
    for name, (base, spread) in spreads.items():
        noise = np.random.default_rng([zlib.crc32(name.encode()), seed]).standard_normal(out[name].shape)
        drawn = base * np.exp(spread * noise) if base else spread * noise
        out[name] = jnp.asarray(drawn.astype(out[name].dtype))
    for name, factor in factors.items():
        out[name] = (out[name] * factor).astype(out[name].dtype)
    return out
```

```python
from contextlib import ExitStack

import numpy as np

import concourse.bass as bass
from concourse import mybir

F32 = mybir.dt.float32
F32R = mybir.dt.float32r
I32 = mybir.dt.int32
U32 = mybir.dt.uint32
ACT = mybir.ActivationFunctionType
ALU = mybir.AluOpType
AX = mybir.AxisListType

P = 128
D = 1024
KD = D // P
LAT = 256
TOK = 512
LAYERS = 2
HEADS = 8
QK_HEAD = 96
NOPE = 64
VH = 64
CONV = 512
TAPS = 31
PAD = TAPS // 2
GATES = 3
FF = 2816
FF_TILES = FF // P
FF_GROUPS = (8, 8, 6)
EXPERTS = 8
FFE = 3584
SLOTS = 128
CH = 1024
RAW = 4
SPLIT = 3
TAPS_CA = (5, 5, 5, 5)
TAPS_UNIT = (2, 3)
TAPS_GV = 5
SCALE = QK_HEAD ** -0.5
RMS_EPS = 1e-6
LN_EPS = 1e-5

PARAMS = (("b_mod", 48), ("norm_g", 32), ("b_gate", 24), ("conv_dw", 4 * TAPS), ("conv_db", 4),
          ("conv_ln_g", 4), ("conv_ln_b", 4), ("q_norm_g", 3), ("kv_norm_g", 2), ("gmlp_ln_g", 4),
          ("gmlp_ln_b", 4))
PCOL = {}
NPAR = 0
for _n, _w in PARAMS:
    PCOL[_n] = NPAR
    NPAR += _w

QUARTERS = 4
HN = FFE // 8
KQ = FFE // QUARTERS // P
STEPS = [("a", 0, 1), ("g", 0, 1)]
for _q in range(1, QUARTERS):
    STEPS += [("a", _q, 0), ("turn", _q - 1, 0), ("g", _q, 0), ("w2", _q - 1, 0), ("w2", _q - 1, 1),
              ("a", _q, 1), ("g", _q, 1)]
STEPS.insert(-2, ("gather", 0, 0))
STEPS += [("turn", QUARTERS - 1, 0), ("a", QUARTERS, 0), ("g", QUARTERS, 0), ("w2", QUARTERS - 1, 0),
          ("w2", QUARTERS - 1, 1)]
ECHUNKS = [(*_s, _p) for _s in STEPS if _s[0] in ("a", "g", "w2") for _p in range(2)]
EPRE = 4
EFIRST = ECHUNKS.index(("a", QUARTERS, 0, 0))
ECH = KD // 2 * HN
EN = 12 * QUARTERS
ERAW = 6
ESPLIT = 6
BLOCKS_MIN, BLOCKS_MAX = 4, 11
BLOCKS = BLOCKS_MAX + 1


MOD_FIRST = (4, 0)


def plan():
    chunks, accs = [], []
    between = {L: [("mod", L, n, kp) for n in range(MOD_FIRST[L], 12) for kp in range(4)] for L in range(LAYERS)}

    def mod_between(L):
        if between[L]:
            chunks.append(between[L].pop(0))

    for L in range(LAYERS):
        for n in range(MOD_FIRST[L]):
            chunks += [("mod", L, n, kp) for kp in range(4)]
            accs.append(("mod", L, n))
        for t in ("kv0", "kv1", "kr", "q0", "q1", "q2"):
            chunks.append((t, L))
            accs.append((t, L))
        for i in range(4):
            for s in ("cg", "ca"):
                chunks.append((s, L, i))
                accs.append((s, L, i))
        chunks.append(("uk", L))
        accs += [("uk", L, j) for j in range(4)]
        chunks.append(("uv", L))
        accs += [("uv", L, t) for t in range(4)]
        for j in range(4):
            chunks.append(("uq", L, j))
            accs += [("uq", L, j, h) for h in range(2)]
        for s in ("gv", "gu"):
            for i in range(4):
                chunks.append((s, L, i))
                accs.append((s, L, i))
        for f in range(8):
            for key, fed in [(("gate", L, f, b), [("gate", L, f, b)]) for b in range(3)] + [
                    (("br", L, f), [("br", L, f, 0), ("br", L, f, 1)]), (("brg", L, f), [("br", L, f, 2)])]:
                chunks.append(key)
                accs += fed
                if L == 0 and f:
                    mod_between(0)
        for f in range(8):
            chunks.append(("out", L, f))
            accs.append(("out", L, f))
        if L == 0:
            k0 = 0
            for g, n in enumerate(FF_GROUPS):
                for k in range(k0, k0 + n):
                    for s in ("fa", "fg"):
                        chunks.append((s, k))
                        accs.append((s, k))
                        mod_between(1)
                for f in range(8):
                    chunks.append(("f2", g, f))
                    accs.append(("f2", g, f))
                    mod_between(1)
                k0 += n
    parts = [a for a in accs if (a[0] in ("uk", "uv") and a[2] < 3) or (a[0] == "uq" and a[3] == 0)
             or (a[0] == "br" and a[3] == 0)]
    return ({c: i for i, c in enumerate(chunks)}, {a: i for i, a in enumerate(accs)},
            {a: i for i, a in enumerate(parts)})


CHUNK, ACC, PART = plan()
XLO_0 = 8 + 5 + 4 + 4 + 8 + 8 + FF_TILES
SQ_ALL = 2 * (KD + 5 + 4 + 4 + KD + KD) + KD


def stored(c):
    return (c - EFIRST) % EN


class Counts:

    def __init__(self):
        self.n = {}

    def next(self, s, k=1):
        self.n[s] = self.n.get(s, 0) + k
        return self.n[s]


def build(nc, A, out):
    with ExitStack() as ctx:
        at = [16512]

        def place(name, shape, dt, where=None):
            size = 4 * int(np.prod(shape[1:]))
            if where is None:
                where = at[0]
                at[0] += (size + 31) // 32 * 32
            return nc.alloc_sbuf_tensor_at(name, shape, dt, offset=where)

        def sem(name):
            return ctx.enter_context(nc.semaphore(name))

        hres = place("hres", [P, KD, TOK], F32)
        par = [place(f"par{L}", [P, NPAR], F32) for L in range(LAYERS)]
        ident = place("ident", [P, P], F32)
        ones = place("ones", [P, P], F32)
        rope = place("rope", [P, LAT], F32)
        sel2 = place("sel2", [4, 2], F32)
        modT = place("modT", [P, 2, 48], F32)
        modc = place("modc", [P, 4, 2, 8], F32)
        eps = place("eps", [P, 2], F32)
        rstd = place("rstd", [P, TOK], F32)
        rdiag = rstd[:, 0:2 * P].rearrange("p (t q) -> p t q", t=2)
        std = place("std", [P, TOK], F32)
        rcol = place("rcol", [P, 2], F32)
        fin_sq = place("fin_sq", [P, 2], F32)
        wsT = place("wsT", [P, 8, P], F32)
        bsp = place("bsp", [P, 4, P], F32)
        negmax = place("negmax", [P, 2], F32)
        rsum = place("rsum", [P, 2], F32)
        rinv = place("rinv", [P, 2], F32)
        rowmax = place("rowmax", [P, 2], F32)
        cs32 = place("cs32", [P, KD, 2], F32)
        c4 = place("c4", [P, KD, 4], F32R)
        base = at[0]
        raw = [place(f"raw{i}", [P, CH], F32) for i in range(RAW)]
        whi = [place(f"whi{i}", [P, CH], F32R) for i in range(SPLIT)]
        wlo = [place(f"wlo{i}", [P, CH], F32R) for i in range(SPLIT)]
        ah = place("ah", [P, KD, TOK], F32R)
        al = place("al", [P, KD, TOK], F32R)
        u0 = at[0]
        uch = place("uch", [P, 4, TOK], F32R)
        ucl = place("ucl", [P, 4, TOK], F32R)
        cacc = place("cacc", [P, 4, TOK], F32, u0 + 8192)
        oh = place("oh", [P, 4, TOK], F32R)
        ol = place("ol", [P, 4, TOK], F32R)
        gm0 = at[0]
        gmh = place("gmh", [P, 4, TOK], F32R)
        gml = place("gml", [P, 4, TOK], F32R)
        at[0] = gm0
        cnh = place("cnh", [P, 5, TOK], F32R)
        cnl = place("cnl", [P, 5, TOK], F32R)
        w0 = at[0]
        t16 = place("t16", [P, KD, TOK], F32, w0)
        modrow = [place(f"modrow{i}", [4, 512], F32, u0 + 20480 + 2048 * i) for i in range(2)]
        modrow_g = [place(f"modrow_g{i}", [4, 512], F32, w0 + 34816 + 2048 * i) for i in range(2)]
        UPW = 4 * 2 * (LAT + 2 * PAD) * 4
        up = place("up", [P, 4, 2, LAT + 2 * PAD], F32, w0)
        w1 = w0 + (UPW + 31) // 32 * 32
        c32 = place("c32", [P, 5, TOK], F32, w1)
        sq5 = place("sq5", [P, 5, TOK], F32, w1 + 10240)
        csig = place("csig", [P, 2, TOK], F32, w1 + 20480)
        krt = place("krt", [P, 2, TOK], F32, w1 + 24576)
        kT = place("kT", [QK_HEAD, HEADS, TOK], F32, w1)
        V = place("V", [P, 4, HEADS * VH], F32, w1 + 16384)
        qT = place("qT", [QK_HEAD, 2, TOK], F32, w1 + 24576)
        pr = place("pr", [P, 2, TOK], F32, w1 + 28672)
        pT = place("pT", [P, 2, TOK], F32, w1 + 32768)
        diag = place("diag", [P, 2, P], F32, w1 + 36864)
        uT = place("uT", [P, 4, TOK], F32, w1)
        vT = place("vT", [P, 4, TOK], F32, w1 + 8192)
        vtok = place("vtok", [P, 4, CONV], F32, w1 + 16384)
        sq4 = place("sq4", [P, 4, TOK], F32, w1 + 24576)
        mh = place("mh", [P, KD, TOK], F32R, w0)
        ml = place("ml", [P, KD, TOK], F32R, w0 + 16384)
        gsig = place("gsig", [P, 3, TOK], F32, w1 + 32768)
        msum = place("msum", [P, 2, TOK], F32, w1 + 38912)
        y16 = place("y16", [P, KD, TOK], F32, u0)
        ysq = place("ysq", [P, 2, TOK], F32, u0 + 16384)
        hh = place("hh", [P, KD, TOK], F32R, w0)
        hl = place("hl", [P, KD, TOK], F32R, w0 + 16384)
        fsil = place("fsil", [P, 2, TOK], F32, w0 + 32768)
        fh = place("fh", [P, 2, TOK], F32, w0 + 36864)
        at[0] = base
        eraw = [place(f"eraw{i}", [P, ECH], F32) for i in range(ERAW)]
        ehi = [place(f"ehi{i}", [P, ECH], F32R) for i in range(ESPLIT)]
        elo = [place(f"elo{i}", [P, ECH], F32R) for i in range(ESPLIT)]
        e_ftok = at[0]
        ftok = place("ftok", [P, 2, D], F32)
        xgh = place("xgh", [P, KD, SLOTS], F32R)
        xgl = place("xgl", [P, KD, SLOTS], F32R)
        sact = place("sact", [P, HN], F32)
        r0 = at[0]
        U = place("U", [P, P], F32)
        rw = place("rw", [P, KD, EXPERTS], F32)
        choose = place("choose", [P, BLOCKS, 16], F32)
        prod = place("prod", [P, BLOCKS, 16], F32)
        lg = place("lg", [P, 2, 8], F32)
        top = place("top", [P, 2, 8], F32)
        topi = place("topi", [P, 2, 8], U32)
        topf = place("topf", [P, 2, 8], F32)
        oh1 = place("oh1", [P, 2, 8], F32)
        oh2 = place("oh2", [P, 2, 8], F32)
        mask = place("mask", [P, 2, 8], F32)
        ew = place("ew", [P, 8], F32)
        rr = place("rr", [P, 2, 8], F32)
        rr16 = place("rr16", [P, 2, 16], F32)
        wt16 = place("wt16", [P, 2, 16], F32)
        eid16 = place("eid16", [P, 16], F32)
        valid = place("valid", [P, 16], F32)
        before = [place(f"before{i}", [P, 16], F32) for i in range(2)]
        assert at[0] <= r0 + 4 * 4 * HN
        at[0] = r0
        hq = place("hq", [P, 2, 2 * HN], F32)
        hTh = place("hTh", [P, KQ, SLOTS], F32R)
        hTl = place("hTl", [P, KQ, SLOTS], F32R)
        yh = place("yh", [SLOTS, D], F32R)
        yl = place("yl", [SLOTS, D], F32R)
        macc = place("macc", [P, 2, D], F32)
        S = place("S", [P, 2, SLOTS], F32)
        STr = place("STr", [P, 2, P], F32R)
        iota = place("iota", [P, SLOTS], F32)
        rrp = place("rrp", [P, 2, BLOCKS], F32)
        wtp = place("wtp", [P, 2, BLOCKS], F32)
        ids_f = place("ids_f", [P, BLOCKS], F32)
        ids_i = place("ids_i", [P, BLOCKS], I32)
        niter_i = place("niter_i", [P, 1], I32)
        assert at[0] <= nc.sbuf_usable_end, at[0]
        fT = place("fT", [P, KD, LAT], F32, base)
        msq = place("msq", [P, D], F32, e_ftok)

        ps = [ctx.enter_context(nc.psum_tensor(f"bank{i}", [P, 512], F32)) for i in range(8)]
        acc_bank = ps[0:2]
        STAT, MISC = ps[2], ps[3]
        sc_bank = ps[4:6]
        TB = ps[6]
        o_bank = (ps[7], ps[3])

        const_landed = sem("const_landed")
        xt_landed = sem("xt_landed")
        layer_landed = sem("layer_landed")
        raw_landed = [sem(f"raw_landed{i}") for i in range(RAW)]
        w_hi = sem("w_hi")
        w_lo = sem("w_lo")
        chunk_used = sem("chunk_used")
        part = sem("part")
        acc_free = [sem("acc_free0"), sem("acc_free1")]
        act_chain = sem("act_chain")
        dve_chain = sem("dve_chain")
        c_ready = sem("c_ready")
        modcol_done = sem("modcol_done")
        mod_rows = sem("mod_rows")
        sq_ready = sem("sq_ready")
        mean_psum = sem("mean_psum")
        sumsq_psum = sem("sumsq_psum")
        ysq_used = sem("ysq_used")
        std_ready = sem("std_ready")
        rdiag_ready = sem("rdiag_ready")
        norm_t = sem("norm_t")
        x_hi = sem("x_hi")
        x_lo = sem("x_lo")
        sub_ready = sem("sub_ready")
        sig_ready = sem("sig_ready")
        sc_ready = sem("sc_ready")
        negmax_ready = sem("negmax_ready")
        exp_ready = sem("exp_ready")
        rinv_ready = sem("rinv_ready")
        p_ready = sem("p_ready")
        pt_psum = sem("pt_psum")
        pt_ready = sem("pt_ready")
        o_psum = sem("o_psum")
        o_ready = sem("o_ready")
        vt_ready = sem("vt_ready")
        vt_psum = sem("vt_psum")
        vtok_ready = sem("vtok_ready")
        sp_psum = sem("sp_psum")
        sp_done = sem("sp_done")
        res_ready = sem("res_ready")
        tap_done = [sem(f"tap_done{i}") for i in range(4)]
        conv_sum = sem("conv_sum")
        raw_e = [sem(f"raw_e{i}") for i in range(ERAW)]
        e_hi = sem("e_hi")
        e_lo = sem("e_lo")
        e_used = sem("e_used")
        ft_in = sem("ft_in")
        ft_psum = sem("ft_psum")
        ft_ready = sem("ft_ready")
        log_psum = sem("log_psum")
        lg_ready = sem("lg_ready")
        e_exp = sem("e_exp")
        mask_ready = sem("mask_ready")
        rank_psum = sem("rank_psum")
        niter_ready = sem("niter_ready")
        s_ready = sem("s_ready")
        g_psum = sem("g_psum")
        xg_hi = sem("xg_hi")
        xg_lo = sem("xg_lo")
        st_psum = sem("st_psum")
        st_ready = sem("st_ready")
        silu_done = sem("silu_done")
        h_done = sem("h_done")
        hT_psum = sem("hT_psum")
        hT_hi = sem("hT_hi")
        hT_lo = sem("hT_lo")
        y_hi = sem("y_hi")
        y_lo = sem("y_lo")
        sct_psum = sem("sct_psum")
        sct_done = sem("sct_done")
        mt_psum = sem("mt_psum")
        fin_ready = sem("fin_ready")
        out_landed = sem("out_landed")

        def p_(L, name, i=0, n=1):
            c = PCOL[name] + i
            return par[L][:, c:c + n]

        def streams(n):
            return [(0, LAT, 0)] + ([(LAT, TOK, 1)] if n == TOK else [])

        def live(L):
            return TOK if L < LAYERS - 1 else LAT

        def row_buffer(L, g):
            return (modrow_g if L == 0 and g >= MOD_FIRST[0] else modrow)[g % 2]

        def rows_between():
            rows = [(L, g) for L in range(LAYERS) for g in range(MOD_FIRST[L], 12)]
            return {L: [(g, kp, rows.index((L, g))) for M, g in rows if M == L for kp in range(4)]
                    for L in range(LAYERS)}

        UNITS = {L: [(j, h, t) for j in range(4) for h in range(2) for t in range(live(L) // P)]
                 for L in range(LAYERS)}

        def keys_of(t):
            return (0, TOK) if t < 2 else (LAT, TOK)

        def taken(eng, key):
            a = ACC[key]
            eng.wait_ge(acc_free[a % 2], a // 2 + 1)

        n_const = 7
        block = ctx.enter_context(nc.Block())

        @block.sync
        def _(sp):
            sp.dma_start(cs32[:], A["cvec"]).then_inc(const_landed, 16)
            sp.dma_start(ident[:], A["ident"]).then_inc(const_landed, 16)
            sp.dma_start(ones[:], A["ones"]).then_inc(const_landed, 16)
            sp.dma_start(rope[:], A["rope"]).then_inc(const_landed, 16)
            sp.dma_start(sel2[:], A["sel2"]).then_inc(const_landed, 16)
            for L in range(LAYERS):
                sp.dma_start(par[L][:], A["par"][L]).then_inc(const_landed, 16)
            total = len(CHUNK)
            for c in range(total):
                if c >= RAW:
                    sp.wait_ge(w_lo, c - RAW + 1)
                sp.dma_start(raw[c % RAW][:], A["dense"][c]).then_inc(raw_landed[c % RAW], 16)
                if c == RAW:
                    sp.dma_start(hres[:], A["xT"]).then_inc(xt_landed, 16)
                for L in range(LAYERS):
                    if c == CHUNK[("mod", L, 2, 0)]:
                        if L:
                            sp.wait_ge(sp_done, 4 * L)
                        sp.dma_start(wsT[:], A["wsT"][L]).then_inc(layer_landed, 16)
                        sp.dma_start(bsp[:], A["bsp"][L]).then_inc(layer_landed, 16)
            sp.wait_ge(chunk_used, total)
            sp.dma_start(iota[:], A["iota"]).then_inc(const_landed, 16)
            sp.dma_start(U[:], A["upper"]).then_inc(const_landed, 16)
            sp.dma_start(rw[:], A["rw"]).then_inc(const_landed, 16)
            sp.wait_ge(niter_ready, 1)
            n_iter = sp.value_load(niter_i[0:1, 0:1], min_val=BLOCKS_MIN, max_val=BLOCKS_MAX)
            first = sp.value_load(ids_i[0:1, 0:1], min_val=0, max_val=EXPERTS - 1)

            def fetch(expert, c, place_):
                sp.dma_start(eraw[place_ % ERAW][:], A["moe"][bass.ds(expert, 1), c].rearrange("a p n -> (a p) n")
                             ).then_inc(raw_e[place_ % ERAW], 16)

            for i in range(EPRE + ERAW):
                if i >= ERAW:
                    sp.wait_ge(e_lo, i - ERAW + 1)
                fetch(first, stored(i + (EFIRST if i < EPRE else -EPRE)), i)
            with sp.Fori(0, n_iter) as it:
                this = sp.value_load(ids_i[0:1, bass.ds(it, 1)], min_val=0, max_val=EXPERTS - 1)
                following = sp.value_load(ids_i[0:1, bass.ds(it + 1, 1)], min_val=0, max_val=EXPERTS - 1)
                for c in range(EN):
                    sp.wait_ge(e_lo, it * EN + (EPRE + c + 1))
                    m = c + ERAW
                    of_next = m >= EN or ECHUNKS[m][1] == QUARTERS
                    fetch(following if of_next else this, stored(m), EPRE + m)
            sp.wait_ge(e_lo, n_iter * EN + (EPRE + ERAW))
            for half in range(2):
                sp.wait_ge(fin_ready, KD // 2 * (half + 1))
                ks = slice(KD // 2 * half, KD // 2 * (half + 1))
                sp.dma_start(out[:, ks, :], hres[:, ks, 0:LAT]).then_inc(out_landed, 16)
            sp.wait_ge(out_landed, 32)

        @block.tensor
        def _(pe):
            n = Counts()

            def mm3(dst, wh, wl, xh, xl, first, last):
                pe.matmul(dst, wh, xh, start=first, stop=False, skip_group_check=True)
                pe.matmul(dst, wh, xl, start=False, stop=False, skip_group_check=True)
                return pe.matmul(dst, wl, xh, start=False, stop=last, skip_group_check=True)

            def weights(key):
                c = CHUNK[key]
                pe.wait_ge(w_lo, c + 1)
                return whi[c % SPLIT], wlo[c % SPLIT]

            def bank(key):
                a = ACC[key]
                if a >= 2:
                    pe.wait_ge(acc_free[a % 2], a // 2)
                return acc_bank[a % 2]

            def column_tile(key, xh, xl, nk, ntok, off=0, acc=None, wait_x=None, signal=chunk_used):
                wh, wl = weights(key)
                b = bank(acc or key)
                for k in range(nk):
                    if wait_x is not None:
                        pe.wait_ge(x_lo, wait_x[k])
                    cols = slice(off + k * P, off + (k + 1) * P)
                    mm = mm3(b[:, 0:ntok], wh[:, cols], wl[:, cols], xh[:, k, 0:ntok], xl[:, k, 0:ntok],
                             k == 0, k == nk - 1)
                mm.then_inc(signal, 1)

            def stat_bank():
                if n.n.get(sumsq_psum):
                    pe.wait_ge(std_ready, n.n[sumsq_psum])

            def sum_squares(nk, src, ntok):
                stat_bank()
                for k in range(nk):
                    pe.wait_ge(sq_ready, n.next(sq_ready))
                    mm = pe.matmul(STAT[:, 0:ntok], ones[:], src(k), start=(k == 0), stop=(k == nk - 1))
                mm.then_inc(sumsq_psum, 1)
                n.next(sumsq_psum)

            def mod_product(L, g, kp, b):
                wh, wl = weights(("mod", L, g, kp))
                for kk in range(2):
                    pe.matmul(b[0:4, :], c4[:, 2 * kp + kk, :], wh[:, kk * 512:kk * 512 + 512],
                              start=(kp + kk == 0), stop=False, skip_group_check=True)
                    mm = pe.matmul(b[0:4, :], c4[:, 2 * kp + kk, :], wl[:, kk * 512:kk * 512 + 512],
                                   start=False, stop=(kp == 3 and kk == 1), skip_group_check=True)
                mm.then_inc(chunk_used, 1)

            def turn_rows(L, g):
                for j in range(4):
                    m = 4 * g + j
                    mm = pe.matmul(MISC[:, 2 * m:2 * m + 2], row_buffer(L, g)[:, j * P:(j + 1) * P],
                                   sel2[:], start=True, stop=True, skip_group_check=True)
                mm.then_inc(modcol_done, 1)

            mod_left = rows_between()

            def mod_between(L):
                if not mod_left[L]:
                    return
                g, kp, row = mod_left[L].pop(0)
                if kp == 0 and row >= 2:
                    pe.wait_ge(mod_rows, row - 1)
                mod_product(L, g, kp, sc_bank[g % 2])
                if kp == 3 and g > MOD_FIRST[L]:
                    pe.wait_ge(mod_rows, row)
                    turn_rows(L, g - 1)

            pe.wait_ge(const_landed, 16 * n_const)
            pe.wait_ge(c_ready, 1)
            xl_seen = 0
            for L in range(LAYERS):
                nq = live(L)
                if L == 0:
                    for g in range(MOD_FIRST[0] + 1):
                        if g == 2:
                            sum_squares(KD, lambda k: t16[:, k, :], TOK)
                        if g < MOD_FIRST[0]:
                            b = bank(("mod", L, g))
                            for kp in range(4):
                                mod_product(L, g, kp, b)
                        if g >= 1:
                            taken(pe, ("mod", L, g - 1))
                            turn_rows(L, g - 1)
                else:
                    pe.wait_ge(mod_rows, 24 - MOD_FIRST[0])
                    turn_rows(L, 11)
                    sum_squares(KD, lambda k: t16[:, k, :], TOK)
                xw = [xl_seen + k + 1 for k in range(KD)]
                xl_seen += KD
                column_tile(("kv0", L), ah, al, KD, TOK, wait_x=xw)
                for t in ("kv1", "kr"):
                    column_tile((t, L), ah, al, KD, TOK)
                for t in ("q0", "q1", "q2"):
                    column_tile((t, L), ah, al, KD, nq)
                for i in range(4):
                    column_tile(("cg", L, i), ah, al, KD, nq)
                    column_tile(("ca", L, i), ah, al, KD, nq)
                    if i == 0:
                        sum_squares(2, lambda k: sq5[:, k, :], TOK)
                    if i == 1:
                        sum_squares(3, lambda k: sq5[:, 2 + k, 0:nq], nq)
                pe.wait_ge(x_lo, xl_seen + 2)
                wh, wl = weights(("uk", L))
                for j in range(4):
                    b = bank(("uk", L, j))
                    for k in range(2):
                        cols = slice(k * 512 + j * P, k * 512 + (j + 1) * P)
                        mm = mm3(b[:], wh[:, cols], wl[:, cols], cnh[:, k, :], cnl[:, k, :], k == 0, k == 1)
                    mm.then_inc(chunk_used if j == 3 else part, 1)
                wh, wl = weights(("uv", L))
                for t in range(4):
                    b = bank(("uv", L, t))
                    ts = slice(t * P, (t + 1) * P)
                    for k in range(2):
                        mm = mm3(b[:], cnh[:, k, ts], cnl[:, k, ts], wh[:, k * 512:(k + 1) * 512],
                                 wl[:, k * 512:(k + 1) * 512], k == 0, k == 1)
                    mm.then_inc(chunk_used if t == 3 else part, 1)
                xl_seen += 5
                pe.wait_ge(x_lo, xl_seen)
                units = UNITS[L]

                def scores(u):
                    j, h, t = units[u]
                    if (h, t) == (0, 0):
                        wh, wl = weights(("uq", L, j))
                        for hh_ in range(2):
                            b = bank(("uq", L, j, hh_))
                            for k in range(3):
                                cols = slice((k * 2 + hh_) * P, (k * 2 + hh_ + 1) * P)
                                mm = mm3(b[:, 0:nq], wh[:, cols], wl[:, cols], cnh[:, 2 + k, 0:nq],
                                         cnl[:, 2 + k, 0:nq], k == 0, k == 2)
                            mm.then_inc(chunk_used if hh_ else part, 1)
                        taken(pe, ("uv", L, 3))
                        taken(pe, ("uq", L, j, 1))
                    if base_u + u >= 2:
                        pe.wait_ge(exp_ready, base_u + u - 1)
                    lo, hi = keys_of(t)
                    pe.matmul(sc_bank[u % 2][:, 0:hi - lo], qT[:, h, t * P:(t + 1) * P],
                              kT[:, 2 * j + h, lo:hi], start=True, stop=True).then_inc(sc_ready, 1)

                def turn(u):
                    lo, hi = keys_of(units[u][2])
                    pe.wait_ge(p_ready, base_u + u + 1)
                    if base_u + u:
                        pe.wait_ge(pt_ready, base_u + u)
                    for i in range((hi - lo) // P):
                        mm = pe.matmul(TB[:, i * P:(i + 1) * P], pr[:, u % 2, i * P:(i + 1) * P], diag[:, u % 2, :],
                                       start=True, stop=True, skip_group_check=True)
                    mm.then_inc(pt_psum, 1)

                def values(u):
                    j, h, t = units[u]
                    lo, hi = keys_of(t)
                    nk = (hi - lo) // P
                    pe.wait_ge(pt_ready, base_u + u + 1)
                    if base_u + u >= 2:
                        pe.wait_ge(o_ready, base_u + u - 1)
                    for i in range(nk):
                        mm = pe.matmul(o_bank[u % 2][64 * h:64 * h + 64, 0:P],
                                       V[:, lo // P + i, (2 * j + h) * VH:(2 * j + h + 1) * VH],
                                       pT[:, u % 2, i * P:(i + 1) * P], start=(i == 0), stop=(i == nk - 1))
                    mm.then_inc(o_psum, 1)

                base_u = 0 if L == 0 else len(UNITS[0])
                for s in range(len(units) + 3):
                    if s < len(units):
                        scores(s)
                    if 2 <= s <= len(units) + 1:
                        turn(s - 2)
                    if s >= 3:
                        values(s - 3)
                for i in range(4):
                    column_tile(("gv", L, i), ah, al, KD, nq)
                for i in range(4):
                    column_tile(("gu", L, i), ah, al, KD, nq)
                    if i == 0:
                        stat_bank()
                        taken(pe, ("gv", L, 3))
                        for k in range(4):
                            mm = pe.matmul(STAT[:, 0:nq], ones[:], vT[:, k, 0:nq], start=(k == 0), stop=(k == 3))
                        mm.then_inc(mean_psum, 1)
                    if i == 1:
                        sum_squares(4, lambda k: sq4[:, k, 0:nq], nq)
                stat_bank()
                for k in range(4):
                    pe.wait_ge(conv_sum, 4 * L + k + 1)
                    mm = pe.matmul(STAT[:, 0:nq], ones[:], cacc[:, k, 0:nq], start=(k == 0), stop=(k == 3))
                mm.then_inc(mean_psum, 1)
                for c in range(nq // P):
                    if c == 0:
                        pe.wait_ge(vt_ready, 8 * L + 4)
                    else:
                        pe.wait_ge(vtok_ready, n.next(vtok_ready))
                    for i in range(4):
                        mm = pe.transpose(TB[:, i * P:(i + 1) * P], vT[:, i, c * P:(c + 1) * P], ident[:])
                    mm.then_inc(vt_psum, 1)
                pe.wait_ge(vtok_ready, n.next(vtok_ready))
                pe.wait_ge(layer_landed, 16 * 2 * (L + 1))
                for i in range(4):
                    if L or i >= 2:
                        pe.wait_ge(sp_done, 4 * L + i - 1)
                    for c in range(nq // P):
                        for g in range(2):
                            mm = pe.matmul(sc_bank[i % 2][64 * g:64 * g + 64, c * P:(c + 1) * P],
                                           vtok[:, c, (2 * i + g) * 64:(2 * i + g + 1) * 64], wsT[:, 2 * i + g, :],
                                           start=True, stop=True, skip_group_check=True)
                    mm.then_inc(sp_psum, 1)
                xl_seen += 8
                for f in range(8):
                    for b_ in range(3):
                        column_tile(("gate", L, f, b_), ah, al, KD, nq)
                        if L == 0 and f:
                            mod_between(0)
                        if (f, b_) == (0, 0):
                            sum_squares(4, lambda k: sq4[:, k, 0:nq], nq)
                    if f == 0:
                        pe.wait_ge(x_lo, xl_seen)
                    column_tile(("br", L, f), uch, ucl, 4, nq, acc=("br", L, f, 0), signal=part)
                    column_tile(("br", L, f), oh, ol, 4, nq, off=512, acc=("br", L, f, 1))
                    if L == 0 and f:
                        mod_between(0)
                    column_tile(("brg", L, f), gmh, gml, 4, nq, acc=("br", L, f, 2))
                    if L == 0 and f:
                        mod_between(0)
                if L == 0:
                    pe.wait_ge(mod_rows, 12 - MOD_FIRST[0])
                    turn_rows(L, 11)
                xw = [xl_seen + k + 1 for k in range(KD)]
                xl_seen += KD
                for f in range(8):
                    column_tile(("out", L, f), mh, ml, KD, nq, wait_x=xw if f == 0 else None)
                    if f == 1:
                        stat_bank()
                    if f >= 1:
                        pe.wait_ge(sq_ready, n.next(sq_ready))
                        pe.matmul(STAT[:, 0:nq], ones[:], ysq[:, (f - 1) % 2, 0:nq], start=(f == 1), stop=False,
                                  skip_group_check=True).then_inc(ysq_used, 1)
                pe.wait_ge(sq_ready, n.next(sq_ready))
                pe.matmul(STAT[:, 0:nq], ones[:], ysq[:, 1, 0:nq], start=False, stop=True,
                          skip_group_check=True).then_inc(sumsq_psum, 1)
                n.next(sumsq_psum)
                sum_squares(KD, lambda k: t16[:, k, 0:nq], nq)
                if L == 0:
                    xw = [xl_seen + k + 1 for k in range(KD)]
                    xl_seen += KD
                    k0 = 0
                    for g, ng in enumerate(FF_GROUPS):
                        for k in range(k0, k0 + ng):
                            column_tile(("fa", k), ah, al, KD, TOK, wait_x=xw if k == 0 else None)
                            mod_between(1)
                            column_tile(("fg", k), ah, al, KD, TOK)
                            mod_between(1)
                        xw2 = [xl_seen + i + 1 for i in range(ng)]
                        xl_seen += ng
                        for f in range(8):
                            column_tile(("f2", g, f), hh, hl, ng, TOK, wait_x=xw2 if f == 0 else None)
                            mod_between(1)
                            if g == 2 and f == 1:
                                stat_bank()
                            if g == 2 and f >= 1:
                                pe.wait_ge(sq_ready, n.next(sq_ready))
                                pe.matmul(STAT[:], ones[:], fh[:, (f - 1) % 2, :], start=(f == 1), stop=False,
                                          skip_group_check=True).then_inc(ysq_used, 1)
                        k0 += ng
                    pe.wait_ge(sq_ready, n.next(sq_ready))
                    pe.matmul(STAT[:], ones[:], fh[:, 1, :], start=False, stop=True,
                              skip_group_check=True).then_inc(sumsq_psum, 1)
                    n.next(sumsq_psum)

            pe.wait_ge(const_landed, 16 * (n_const + 3))
            pe.wait_ge(ft_in, KD)
            for t in range(2):
                for k in range(KD):
                    mm = pe.matmul(MISC[:, 8 * t:8 * t + 8], fT[:, k, t * P:(t + 1) * P], rw[:, k, :],
                                   start=(k == 0), stop=(k == KD - 1), skip_group_check=True)
            mm.then_inc(log_psum, 1)
            for t in range(2):
                for half in range(2):
                    for i in range(4):
                        k = 4 * half + i
                        mm = pe.transpose(ps[4 + 2 * t + half][:, i * P:(i + 1) * P], fT[:, k, t * P:(t + 1) * P],
                                          ident[:])
                    mm.then_inc(ft_psum, 1)
            pe.wait_ge(mask_ready, 1)
            stat_bank()
            pe.matmul(STAT[:, 0:8], U[:], mask[:, 0, :], start=True, stop=True, skip_group_check=True)
            pe.matmul(STAT[:, 8:16], ones[:], mask[:, 0, :], start=True, stop=False, skip_group_check=True)
            pe.matmul(STAT[:, 8:16], U[:], mask[:, 1, :], start=False, stop=True, skip_group_check=True)
            pe.matmul(STAT[:, 16:24], ones[:], mask[:, 0, :], start=True, stop=False, skip_group_check=True)
            pe.matmul(STAT[:, 16:24], ones[:], mask[:, 1, :], start=False, stop=True,
                      skip_group_check=True).then_inc(rank_psum, 1)
            pe.wait_ge(niter_ready, 1)
            n_iter = pe.value_load(niter_i[0:1, 0:1], min_val=BLOCKS_MIN, max_val=BLOCKS_MAX)
            pe.wait_ge(ft_ready, 4)

            def gather():
                for half in range(2):
                    for i in range(4):
                        k = 4 * half + i
                        for t in range(2):
                            mm = pe.matmul(ps[6 + half][:, i * P:(i + 1) * P], ftok[:, t, k * P:(k + 1) * P],
                                           S[:, t, :], start=(t == 0), stop=(t == 1), skip_group_check=True)
                    mm.then_inc(g_psum, 1)

            def product13(which, it, c, count):
                if count is not None:
                    pe.wait_ge((silu_done, h_done)[which], count)
                for k in range(KD):
                    if k % 4 == 0:
                        pe.wait_ge(e_lo, it * EN + (c + k // 4 + 1))
                    wh, wl = ehi[(c + k // 4) % ESPLIT], elo[(c + k // 4) % ESPLIT]
                    cols = slice(k % 4 * HN, (k % 4 + 1) * HN)
                    mm = mm3(acc_bank[which][:, 0:HN], xgh[:, k, :], xgl[:, k, :], wh[:, cols], wl[:, cols],
                             k == 0, k == KD - 1)
                    if k % 4 == 3:
                        mm.then_inc(e_used, 1)

            def turn_slots():
                for t in range(2):
                    mm = pe.transpose(MISC[:, t * P:(t + 1) * P], S[:, t, :], ident[:])
                mm.then_inc(st_psum, 1)

            pe.wait_ge(s_ready, 1)
            gather()
            turn_slots()
            pe.wait_ge(xg_lo, 2)
            product13(0, 0, 0, None)
            product13(1, 0, 2, None)
            with pe.Fori(0, n_iter) as it:
                c = EPRE
                for kind, q, half in STEPS:
                    if kind == "gather":
                        pe.wait_ge(s_ready, it + 2)
                        gather()
                        continue
                    if kind == "turn":
                        pe.wait_ge(h_done, it * 8 + (2 * q + 2))
                        for i in range(KQ):
                            mm = pe.transpose(ps[4 + i // 4][:, (i % 4) * P:(i % 4 + 1) * P],
                                              hq[:, q % 2, i * P:(i + 1) * P], ident[:])
                        mm.then_inc(hT_psum, 1)
                        continue
                    if kind == "w2":
                        if half == 0:
                            pe.wait_ge(hT_lo, it * 4 + (q + 1))
                            if q == 0:
                                pe.wait_ge(st_ready, it + 1)
                        for p in range(2):
                            pe.wait_ge(e_lo, it * EN + (c + p + 1))
                            wh, wl = ehi[(c + p) % ESPLIT], elo[(c + p) % ESPLIT]
                            y = (STAT, MISC)[half][:, p * 256:(p + 1) * 256]
                            for k in range(KQ):
                                cols = slice(k * 256, (k + 1) * 256)
                                mm = mm3(y, hTh[:, k, :], hTl[:, k, :], wh[:, cols], wl[:, cols],
                                         q == 0 and k == 0 and p == 0, q == QUARTERS - 1 and k == KQ - 1)
                            mm.then_inc(e_used, 1)
                    else:
                        if (kind, q) == ("a", QUARTERS):
                            pe.wait_ge(xg_lo, it * 2 + 4)
                        product13(("a", "g").index(kind), it, c, it * 8 + (2 * q + half))
                    c += 2
                for half in range(2):
                    pe.wait_ge(y_lo, it * 2 + (half + 1))
                    for t in range(2):
                        b = ps[4 + t]
                        if half:
                            pe.wait_ge(sct_done, it * 4 + (t + 1))
                        cols = slice(half * 512, half * 512 + 512)
                        pe.matmul(b[:], STr[:, t, :], yh[:, cols], start=True, stop=False, skip_group_check=True)
                        pe.matmul(b[:], STr[:, t, :], yl[:, cols], start=False, stop=True,
                                  skip_group_check=True).then_inc(sct_psum, 1)
                turn_slots()
            pe.wait_ge(rdiag_ready, 1)
            for pair in range(4):
                for i in range(2):
                    k = 2 * pair + i
                    for t in range(2):
                        mm = pe.matmul(ps[4 + pair][:, i * LAT + t * P:i * LAT + (t + 1) * P],
                                       macc[:, t, k * P:(k + 1) * P], rdiag[:, t, :], start=True, stop=True,
                                       skip_group_check=True)
                mm.then_inc(mt_psum, 1)

        @block.scalar
        def _(act):
            n = Counts()
            hi_done = [0]

            def round_to(c_last):
                while hi_done[0] <= min(c_last, len(CHUNK) - 1):
                    c = hi_done[0]
                    act.wait_ge(raw_landed[c % RAW], 16 * (c // RAW + 1))
                    if c >= SPLIT:
                        act.wait_ge(chunk_used, c - SPLIT + 1)
                    nc.scalar.copy(whi[c % SPLIT][:], raw[c % RAW][:]).then_inc(w_hi, 1)
                    hi_done[0] += 1

            def chain(ins):
                ins.then_inc(act_chain, 1)
                act.wait_ge(act_chain, n.next(act_chain))

            def await_acc(key, chunk=None):
                round_to(CHUNK[chunk or key] + 2)
                act.wait_ge(chunk_used, CHUNK[chunk or key] + 1)
                return acc_bank[ACC[key] % 2], acc_free[ACC[key] % 2]

            def await_part(key, chunk):
                round_to(CHUNK[chunk] + 1)
                act.wait_ge(part, PART[key] + 1)
                return acc_bank[ACC[key] % 2], acc_free[ACC[key] % 2]

            def root(ntok, inv_n, which):
                act.wait_ge(sumsq_psum, n.next(sumsq_psum))
                nc.scalar.activation(std[:, 0:ntok], STAT[:, 0:ntok], ACT.Sqrt, bias=eps[:, which:which + 1],
                                     scale=inv_n).then_inc(std_ready, 1)

            def affine_hi(which, ntok, dst):
                for k in range(KD):
                    for lo, hi, s in streams(ntok):
                        act.wait_ge(norm_t, n.next(norm_t))
                        nc.scalar.activation(dst[:, k, lo:hi], t16[:, k, lo:hi], ACT.Identity,
                                             bias=modT[:, s, 24 * which + k:24 * which + k + 1]).then_inc(x_hi, 1)

            def pre_squares():
                for k in range(KD):
                    nc.scalar.activation(t16[:, k, :], hres[:, k, :], ACT.Square).then_inc(sq_ready, 1)

            mod_left = rows_between()

            def mod_between(L):
                if not mod_left[L]:
                    return
                g, kp, row = mod_left[L].pop(0)
                c = CHUNK[("mod", L, g, kp)]
                round_to(c + 2)
                if kp == 3:
                    act.wait_ge(chunk_used, c + 1)
                    act.wait_ge(modcol_done, 12 * L + g - 1)
                    nc.scalar.copy(row_buffer(L, g)[:], sc_bank[g % 2][0:4, :]).then_inc(mod_rows, 1)

            act.wait_ge(const_landed, 16 * n_const)
            chain(nc.scalar.activation(cs32[:], cs32[:], ACT.Silu))
            nc.scalar.copy(c4[:, :, 0:2], cs32[:]).then_inc(x_hi, 1)
            round_to(1)
            for L in range(LAYERS):
                nq = live(L)
                for g in range(MOD_FIRST[L]):
                    if g == 2:
                        act.wait_ge(xt_landed, 16)
                        pre_squares()
                    for kp in range(4):
                        round_to(CHUNK[("mod", L, g, kp)] + 2)
                    b, free = await_acc(("mod", L, g), ("mod", L, g, 3))
                    if g >= 2:
                        act.wait_ge(modcol_done, g - 1)
                    nc.scalar.copy(modrow[g % 2][:], b[0:4, :]).then_inc(free, 1)
                if L:
                    act.wait_ge(res_ready, n.next(res_ready, KD))
                    pre_squares()
                root(TOK, 1.0 / D, 0)
                affine_hi(0, TOK, ah)
                def low_rank(t, name, ntok):
                    b, free = await_acc((name, L))
                    nc.scalar.copy(c32[:, t, 0:ntok], b[:, 0:ntok]).then_inc(free, 1)
                    act.wait_ge(free, ACC[(name, L)] // 2 + 1)
                    nc.scalar.activation(sq5[:, t, 0:ntok], c32[:, t, 0:ntok], ACT.Square).then_inc(sq_ready, 1)

                low_rank(0, "kv0", TOK)
                low_rank(1, "kv1", TOK)
                b, free = await_acc(("kr", L))
                nc.scalar.copy(krt[64:96, 0, LAT:TOK], b[64:96, LAT:TOK]).then_inc(sig_ready, 1)
                for t in range(3):
                    low_rank(2 + t, f"q{t}", nq)

                def low_norm(tiles, ntok, g_name):
                    for t in tiles:
                        act.wait_ge(norm_t, n.next(norm_t))
                        nc.scalar.copy(cnh[:, t, 0:ntok], sq5[:, t, 0:ntok]).then_inc(x_hi, 1)

                for i in range(4):
                    b, free = await_acc(("cg", L, i))
                    if i >= 2:
                        taken(act, ("ca", L, i - 2))
                    nc.scalar.activation(csig[:, i % 2, 0:nq], b[:, 0:nq], ACT.Sigmoid).then_inc(free, 1)
                    round_to(CHUNK[("ca", L, i)] + 2)
                    if i == 1:
                        root(TOK, 1.0 / 256, 0)
                        low_norm((0, 1), TOK, "kv_norm_g")
                    if i == 2:
                        root(nq, 1.0 / 384, 0)
                        low_norm((2, 3, 4), nq, "q_norm_g")
                act.wait_ge(x_lo, XLO_0 * L + 13)
                taken(act, ("ca", L, 3))
                for j in range(4):
                    key = ("uk", L, j)
                    b, free = await_part(key, ("uk", L)) if j < 3 else await_acc(key, ("uk", L))
                    chain(nc.scalar.copy(kT[0:64, 2 * j, :], b[0:64, :]))
                    nc.scalar.copy(kT[0:64, 2 * j + 1, :], b[64:128, :]).then_inc(free, 1)
                taken(act, ("kr", L))
                chain(nc.scalar.copy(kT[64:96, :, :], krt[64:96, 0:1, :].broadcast_to([32, HEADS, TOK])))
                for t in range(4):
                    key = ("uv", L, t)
                    b, free = await_part(key, ("uv", L)) if t < 3 else await_acc(key, ("uv", L))
                    nc.scalar.copy(V[:, t, :], b[:]).then_inc(free, 1)
                units = UNITS[L]
                base_u = 0 if L == 0 else len(UNITS[0])
                for s in range(len(units) + 3):
                    if s < len(units):
                        j, h, t = units[s]
                        if (h, t) == (0, 0):
                            for hh_ in range(2):
                                key = ("uq", L, j, hh_)
                                b, free = (await_acc if hh_ else await_part)(key, ("uq", L, j))
                                if nq == TOK:
                                    nc.scalar.copy(qT[64:96, hh_, LAT:TOK], b[64:96, LAT:TOK])
                                nc.scalar.copy(qT[0:64, hh_, 0:nq], b[0:64, 0:nq]).then_inc(sig_ready, 1)
                    if 2 <= s <= len(units) + 1:
                        u = s - 2
                        lo, hi = keys_of(units[u][2])
                        act.wait_ge(pt_psum, base_u + u + 1)
                        if base_u + u >= 2:
                            act.wait_ge(o_psum, base_u + u - 1)
                        nc.scalar.copy(pT[:, u % 2, 0:hi - lo], TB[:, 0:hi - lo]).then_inc(pt_ready, 1)
                    if 1 <= s <= len(units):
                        u = s - 1
                        act.wait_ge(rinv_ready, base_u + u + 1)
                        if base_u + u >= 2:
                            act.wait_ge(pt_psum, base_u + u - 1)
                        nc.scalar.activation(diag[:, u % 2, :], ident[:], ACT.Copy,
                                             scale=rinv[:, u % 2:u % 2 + 1]).then_inc(p_ready, 1)
                    if s < len(units):
                        lo, hi = keys_of(units[s][2])
                        act.wait_ge(negmax_ready, base_u + s + 1)
                        if base_u + s >= 2:
                            act.wait_ge(pt_psum, base_u + s - 1)
                        nc.scalar.activation(pr[:, s % 2, 0:hi - lo], sc_bank[s % 2][:, 0:hi - lo], ACT.Exp,
                                             bias=negmax[:, s % 2:s % 2 + 1], scale=SCALE,
                                             accum_out=rsum[:, s % 2:s % 2 + 1]).then_inc(exp_ready, 1)
                    if s >= 3:
                        u = s - 3
                        j, h, t = units[u]
                        act.wait_ge(o_psum, base_u + u + 1)
                        nc.scalar.copy(oh[64 * h:64 * h + 64, j, t * P:(t + 1) * P],
                                       o_bank[u % 2][64 * h:64 * h + 64, 0:P]).then_inc(x_hi, 1)
                for i in range(4):
                    b, free = await_acc(("gv", L, i))
                    nc.scalar.activation(vT[:, i, 0:nq], b[:, 0:nq], ACT.Gelu_apprx_tanh).then_inc(free, 1)
                for i in range(4):
                    b, free = await_acc(("gu", L, i))
                    nc.scalar.activation(uT[:, i, 0:nq], b[:, 0:nq], ACT.Gelu_apprx_tanh).then_inc(free, 1)
                    if i == 0:
                        for k in range(4):
                            act.wait_ge(sub_ready, n.next(sub_ready))
                            nc.scalar.activation(sq4[:, k, 0:nq], vT[:, k, 0:nq], ACT.Square).then_inc(sq_ready, 1)
                    if i == 1:
                        root(nq, 1.0 / CONV, 1)
                    if i == 2:
                        for k in range(4):
                            act.wait_ge(norm_t, n.next(norm_t))
                            nc.scalar.activation(vT[:, k, 0:nq], vT[:, k, 0:nq], ACT.Identity,
                                                 bias=p_(L, "gmlp_ln_b", k),
                                                 scale=p_(L, "gmlp_ln_g", k)).then_inc(vt_ready, 1)
                round_to(CHUNK[("gu", L, 3)] + 2)
                for c in range(nq // P):
                    act.wait_ge(vt_psum, n.next(vt_psum))
                    nc.scalar.copy(vtok[:, c, :], TB[:]).then_inc(vtok_ready, 1)
                for i in range(4):
                    act.wait_ge(sub_ready, n.next(sub_ready))
                    nc.scalar.activation(sq4[:, i, 0:nq], cacc[:, i, 0:nq], ACT.Square).then_inc(sq_ready, 1)
                for i in range(4):
                    act.wait_ge(sp_done, 4 * L + i + 1)
                    nc.scalar.copy(gmh[:, i, 0:nq], uT[:, i, 0:nq]).then_inc(x_hi, 1)
                for f in range(8):
                    for b_ in range(3):
                        b, free = await_acc(("gate", L, f, b_))
                        nc.scalar.activation(gsig[:, b_, 0:nq], b[:, 0:nq], ACT.Sigmoid,
                                             bias=p_(L, "b_gate", 8 * b_ + f)).then_inc(free, 1)
                        if L == 0 and f:
                            mod_between(0)
                        if (f, b_) == (0, 0):
                            root(nq, 1.0 / CONV, 1)
                        if (f, b_) == (0, 1):
                            for i in range(4):
                                act.wait_ge(norm_t, n.next(norm_t))
                                nc.scalar.activation(vT[:, i, 0:nq], cacc[:, i, 0:nq], ACT.Silu,
                                                     bias=p_(L, "conv_ln_b", i),
                                                     scale=p_(L, "conv_ln_g", i)).then_inc(vt_ready, 1)
                                act.wait_ge(vt_ready, 8 * L + 4 + i + 1)
                                nc.scalar.copy(uch[:, i, 0:nq], vT[:, i, 0:nq]).then_inc(x_hi, 1)
                    if L == 0 and f:
                        mod_between(0)
                        mod_between(0)
                    round_to(CHUNK[("brg", L, f)] + 2)
                    act.wait_ge(norm_t, n.next(norm_t))
                    nc.scalar.copy(mh[:, f, 0:nq], msum[:, f % 2, 0:nq]).then_inc(x_hi, 1)
                for f in range(8):
                    b, free = await_acc(("out", L, f))
                    nc.scalar.copy(y16[:, f, 0:nq], b[:, 0:nq]).then_inc(free, 1)
                    act.wait_ge(free, ACC[("out", L, f)] // 2 + 1)
                    if f >= 2:
                        act.wait_ge(ysq_used, n.next(ysq_used))
                    nc.scalar.activation(ysq[:, f % 2, 0:nq], y16[:, f, 0:nq], ACT.Square).then_inc(sq_ready, 1)
                n.next(ysq_used, 1)
                root(nq, 1.0 / D, 0)
                for k in range(KD):
                    act.wait_ge(res_ready, n.next(res_ready))
                    nc.scalar.activation(t16[:, k, 0:nq], hres[:, k, 0:nq], ACT.Square).then_inc(sq_ready, 1)
                root(nq, 1.0 / D, 0)
                if L == 0:
                    affine_hi(1, TOK, ah)
                    k0 = 0
                    for g, ng in enumerate(FF_GROUPS):
                        for i in range(ng):
                            k = k0 + i
                            b, free = await_acc(("fa", k))
                            if k >= 2:
                                taken(act, ("fg", k - 2))
                            nc.scalar.activation(fsil[:, k % 2, :], b[:], ACT.Silu).then_inc(free, 1)
                            mod_between(1)
                            round_to(CHUNK[("fg", k)] + 2)
                            taken(act, ("fg", k))
                            nc.scalar.copy(hh[:, i, :], fh[:, k % 2, :]).then_inc(x_hi, 1)
                            mod_between(1)
                        for f in range(8):
                            b, free = await_acc(("f2", g, f))
                            mod_between(1)
                            if g == 2:
                                act.wait_ge(free, ACC[("f2", g, f)] // 2 + 1)
                                if f >= 2:
                                    act.wait_ge(ysq_used, n.next(ysq_used))
                                nc.scalar.activation(fh[:, f % 2, :], y16[:, f, :], ACT.Square).then_inc(sq_ready, 1)
                        k0 += ng
                    n.next(ysq_used, 1)
                    root(TOK, 1.0 / D, 0)
            for k in range(KD):
                act.wait_ge(norm_t, n.next(norm_t))
                nc.scalar.activation(fT[:, k, :], t16[:, k, 0:LAT], ACT.Identity,
                                     bias=modT[:, 0, 24 + k:25 + k]).then_inc(ft_in, 1)
            act.wait_ge(log_psum, 1)
            nc.scalar.copy(lg[:], MISC[:, 0:16].rearrange("p (t e) -> p t e", t=2)).then_inc(lg_ready, 1)
            for t in range(2):
                for half in range(2):
                    act.wait_ge(ft_psum, 2 * t + half + 1)
                    nc.scalar.copy(ftok[:, t, half * 512:half * 512 + 512], ps[4 + 2 * t + half][:]).then_inc(ft_ready, 1)
            act.wait_ge(niter_ready, 1)
            n_iter = act.value_load(niter_i[0:1, 0:1], min_val=BLOCKS_MIN, max_val=BLOCKS_MAX)

            def round_e(it, c):
                act.wait_ge(raw_e[c % ERAW], (it * (EN // ERAW) + (c // ERAW + 1)) * 16)
                if not (isinstance(it, int) and c < ESPLIT):
                    act.wait_ge(e_used, it * EN + (c - ESPLIT + 1))
                nc.scalar.copy(ehi[c % ESPLIT][:], eraw[c % ERAW][:]).then_inc(e_hi, 1)

            def copy_gathered(k):
                for half in range(2):
                    act.wait_ge(g_psum, k + (half + 1))
                    nc.scalar.copy(xgh[:, 4 * half:4 * half + 4, :],
                                   ps[6 + half][:].rearrange("p (k s) -> p k s", k=4)).then_inc(xg_hi, 1)

            def copy_slots(k):
                act.wait_ge(st_psum, k)
                nc.scalar.copy(STr[:], MISC[:, 0:2 * P].rearrange("p (t s) -> p t s", t=2)).then_inc(st_ready, 1)

            def silu(it, c, count):
                act.wait_ge(e_used, it * EN + (c + 2))
                if count is not None:
                    act.wait_ge(h_done, count)
                nc.scalar.activation(sact[:], acc_bank[0][:, 0:HN], ACT.Silu).then_inc(silu_done, 1)

            act.wait_ge(e_exp, 1)
            nc.scalar.activation(ew[:, 2:4], ew[:, 0:2], ACT.Exp).then_inc(e_exp, 1)
            for c in range(ESPLIT):
                round_e(0, c)
            copy_gathered(0)
            copy_slots(1)
            round_e(0, ESPLIT)
            silu(0, 0, None)
            for c in range(ESPLIT + 1, ESPLIT + EPRE):
                round_e(0, c)
            with act.Fori(0, n_iter) as it:
                c = EPRE
                for kind, q, half in STEPS:
                    if kind == "gather":
                        continue
                    if kind == "turn":
                        act.wait_ge(hT_psum, it * 4 + (q + 1))
                        nc.scalar.copy(hTh[:, 0:4, :], ps[4][:].rearrange("p (k s) -> p k s", k=4))
                        nc.scalar.copy(hTh[:, 4:KQ, :], ps[5][:, 0:3 * P].rearrange("p (k s) -> p k s", k=3)
                                       ).then_inc(hT_hi, 1)
                        continue
                    late = (kind, q, half) == ("g", QUARTERS - 1, 1) or (kind, q) == ("w2", QUARTERS - 1)
                    if not late:
                        round_e(it, c + ESPLIT)
                    if kind == "a":
                        silu(it, c, it * 8 + (2 * q + half))
                    if late:
                        act.wait_ge(e_used, it * EN + (c + 2))
                        if kind == "g":
                            copy_gathered(it * 2 + 2)
                        else:
                            nc.scalar.copy(yh[:, half * 512:half * 512 + 512], (STAT, MISC)[half][:]
                                           ).then_inc(y_hi, 1)
                        round_e(it, c + ESPLIT)
                    round_e(it, c + ESPLIT + 1)
                    c += 2
                copy_slots(it + 2)
            for t in range(2):
                act.wait_ge(sct_done, n_iter * 4)
                nc.scalar.activation(msq[:], macc[:, t, :], ACT.Square, accum_out=fin_sq[:, t:t + 1]
                                     ).then_inc(sq_ready, 1)
                act.wait_ge(sq_ready, SQ_ALL + t + 1)
            nc.scalar.activation(std[:, 0:2], fin_sq[:], ACT.Sqrt, bias=eps[:, 0:1], scale=1.0 / D
                                 ).then_inc(std_ready, 1)

        @block.vector
        def _(dve):
            n = Counts()
            lo_done = [0]
            taps_left = []

            def rest_to(c_last):
                while lo_done[0] <= min(c_last, len(CHUNK) - 1):
                    c = lo_done[0]
                    dve.wait_ge(w_hi, c + 1)
                    dve.tensor_tensor(wlo[c % SPLIT][:], raw[c % RAW][:], whi[c % SPLIT][:].bitcast(F32),
                                      ALU.subtract).then_inc(w_lo, 1)
                    lo_done[0] += 1

            def chain(ins):
                ins.then_inc(dve_chain, 1)
                dve.wait_ge(dve_chain, n.next(dve_chain))

            def await_acc(key, chunk=None):
                rest_to(CHUNK[chunk or key] + 2)
                dve.wait_ge(chunk_used, CHUNK[chunk or key] + 1)
                return acc_bank[ACC[key] % 2], acc_free[ACC[key] % 2]

            def await_part(key, chunk):
                rest_to(CHUNK[chunk] + 1)
                dve.wait_ge(part, PART[key] + 1)
                return acc_bank[ACC[key] % 2], acc_free[ACC[key] % 2]

            def invert(ntok):
                dve.wait_ge(std_ready, n.next(std_ready))
                chain(dve.reciprocal(rstd[:, 0:ntok], std[:, 0:ntok]))

            def lo_of(dst, x, hi_part):
                dve.wait_ge(x_hi, n.next(x_hi))
                dve.tensor_tensor(dst, x, hi_part.bitcast(F32), ALU.subtract).then_inc(x_lo, 1)

            def modulated(which, ntok, dst_h, dst_l):
                sts = streams(ntok)
                for k in range(KD + 1):
                    if k < KD:
                        for lo, hi, s in sts:
                            dve.scalar_tensor_tensor(t16[:, k, lo:hi], hres[:, k, lo:hi],
                                                     modc[:, 2 * which, s, k:k + 1], rstd[:, lo:hi],
                                                     ALU.mult, ALU.mult).then_inc(norm_t, 1)
                    if k and dst_l is not None:
                        for i, (lo, hi, s) in enumerate(sts):
                            dve.wait_ge(x_hi, n.next(x_hi))
                            ins = dve.scalar_tensor_tensor(
                                dst_l[:, k - 1, lo:hi], t16[:, k - 1, lo:hi],
                                modT[:, s, 24 * which + k - 1:24 * which + k],
                                dst_h[:, k - 1, lo:hi].bitcast(F32), ALU.add, ALU.subtract)
                            if i == len(sts) - 1:
                                ins.then_inc(x_lo, 1)

            def residual(which, ntok, y):
                for k in range(KD):
                    chain(dve.tensor_tensor(y[:, k, 0:ntok], y[:, k, 0:ntok], rstd[:, 0:ntok], ALU.mult))
                    sts = streams(ntok)
                    for i, (lo, hi, s) in enumerate(sts):
                        ins = dve.scalar_tensor_tensor(hres[:, k, lo:hi], y[:, k, lo:hi],
                                                       modc[:, 2 * which + 1, s, k:k + 1], hres[:, k, lo:hi],
                                                       ALU.mult, ALU.add)
                        if i == len(sts) - 1:
                            ins.then_inc(res_ready, 1)

            def taps(count):
                for _ in range(count):
                    if not taps_left:
                        return
                    L, i, t = min(taps_left[:2], key=lambda x: (x[2], x[1]))
                    taps_left.remove([L, i, t])
                    if t + 1 < TAPS:
                        taps_left.insert(0, [L, i, t + 1])
                    ns = live(L) // LAT
                    src = up[:, i, 0:ns, t:t + LAT]
                    acc = cacc[:, i, 0:ns * LAT].rearrange("p (s t) -> p s t", s=ns)
                    w = p_(L, "conv_dw", TAPS * i + t)
                    if t == 0:
                        ins = dve.tensor_scalar(acc, src, w, p_(L, "conv_db", i), ALU.mult, ALU.add)
                    else:
                        dve.wait_ge(tap_done[i], (TAPS - 1) * L + t)
                        ins = dve.scalar_tensor_tensor(acc, src, w, acc, ALU.mult, ALU.add)
                    ins.then_inc(tap_done[i] if t < TAPS - 1 else conv_sum, 1)

            def modulation(L, lo, hi):
                dve.wait_ge(modcol_done, 12 * L + hi // 4)
                cols = MISC[:, 0:96].rearrange("p (m s) -> p s m", s=2)
                for s in range(2):
                    chain(dve.tensor_tensor(modT[:, s, lo:hi], cols[:, s, lo:hi], p_(L, "b_mod", lo, hi - lo),
                                            ALU.add))
                for s in range(2):
                    for w in range(2):
                        scale, gate = slice(24 * w + 8, 24 * w + 16), slice(24 * w + 16, 24 * w + 24)
                        if lo <= scale.start < hi:
                            chain(dve.scalar_tensor_tensor(modc[:, 2 * w, s, :], modT[:, s, scale], 1.0,
                                                           p_(L, "norm_g", 16 * w, 8), ALU.add, ALU.mult))
                        if lo <= gate.start < hi:
                            chain(dve.tensor_tensor(modc[:, 2 * w + 1, s, :], modT[:, s, gate],
                                                    p_(L, "norm_g", 16 * w + 8, 8), ALU.mult))

            dve.wait_ge(const_landed, 16 * n_const)
            chain(dve.memset(eps[:, 0:1], RMS_EPS))
            chain(dve.memset(eps[:, 1:2], LN_EPS))
            dve.wait_ge(x_hi, n.next(x_hi))
            dve.tensor_tensor(c4[:, :, 2:4], cs32[:], c4[:, :, 0:2].bitcast(F32), ALU.subtract).then_inc(c_ready, 1)
            rest_to(1)
            for L in range(LAYERS):
                nq = live(L)
                for g in range(MOD_FIRST[L]):
                    for kp in range(4):
                        rest_to(CHUNK[("mod", L, g, kp)] + 2)
                modulation(L, 0, 16 if L == 0 else 48)
                invert(TOK)
                if L == 0:
                    dve.wait_ge(xt_landed, 16)
                modulated(0, TOK, ah, al)
                chain(dve.memset(up[:, :, :, 0:PAD], 0.0))
                chain(dve.memset(up[:, :, :, PAD + LAT:], 0.0))
                for t in ("kv0", "kv1"):
                    rest_to(CHUNK[(t, L)] + 2)
                b, free = await_acc(("kr", L))
                dve.wait_ge(sig_ready, n.next(sig_ready))
                chain(dve.tensor_tensor(krt[64:96, 1, 0:LAT], b[96:128, 0:LAT], rope[96:128, :], ALU.mult))
                chain(dve.tensor_tensor(krt[64:96, 0, 0:LAT], b[64:96, 0:LAT], rope[64:96, :], ALU.mult))
                dve.tensor_tensor(krt[64:96, 0, 0:LAT], krt[64:96, 0, 0:LAT], krt[64:96, 1, 0:LAT],
                                  ALU.add).then_inc(free, 1)
                for t in range(3):
                    rest_to(CHUNK[(f"q{t}", L)] + 2)

                def low_norm(tiles, ntok, name):
                    invert(ntok)
                    for i, t in enumerate(tiles):
                        dve.scalar_tensor_tensor(sq5[:, t, 0:ntok], c32[:, t, 0:ntok], p_(L, name, i),
                                                 rstd[:, 0:ntok], ALU.mult, ALU.mult).then_inc(norm_t, 1)
                    dve.wait_ge(norm_t, n.next(norm_t, len(tiles)))
                    for i, t in enumerate(tiles):
                        lo_of(cnl[:, t, 0:ntok], sq5[:, t, 0:ntok], cnh[:, t, 0:ntok])

                for i in range(4):
                    rest_to(CHUNK[("cg", L, i)] + 2)
                    b, free = await_acc(("ca", L, i))
                    taken(dve, ("cg", L, i))
                    ns = nq // LAT
                    dve.tensor_tensor(up[:, i, 0:ns, PAD:PAD + LAT],
                                      b[:, 0:nq].rearrange("p (s t) -> p s t", s=ns),
                                      csig[:, i % 2, 0:nq].rearrange("p (s t) -> p s t", s=ns),
                                      ALU.mult).then_inc(free, 1)
                    taken(dve, ("ca", L, i))
                    taps_left.append([L, i, 0])
                    taps(TAPS_CA[i])
                    if i == 1:
                        low_norm((0, 1), TOK, "kv_norm_g")
                    if i == 2:
                        low_norm((2, 3, 4), nq, "q_norm_g")
                rest_to(CHUNK[("uk", L)] + 2)
                rest_to(CHUNK[("uv", L)] + 2)
                units = UNITS[L]
                base_u = 0 if L == 0 else len(UNITS[0])
                for s in range(len(units) + 4):
                    if s < len(units):
                        j, h, t = units[s]
                        if (h, t) == (0, 0):
                            for hh_ in range(2):
                                key = ("uq", L, j, hh_)
                                b, free = (await_acc if hh_ else await_part)(key, ("uq", L, j))
                                dve.wait_ge(sig_ready, n.next(sig_ready))
                                chain(dve.tensor_tensor(rstd[64:96, 0:LAT], b[96:128, 0:LAT], rope[96:128, :], ALU.mult))
                                chain(dve.tensor_tensor(rstd[64:96, LAT:TOK], b[64:96, 0:LAT], rope[64:96, :], ALU.mult))
                                dve.tensor_tensor(qT[64:96, hh_, 0:LAT], rstd[64:96, 0:LAT], rstd[64:96, LAT:TOK],
                                                  ALU.add).then_inc(free, 1)
                                taken(dve, key)
                    if 1 <= s <= len(units):
                        u = s - 1
                        i = u % 2
                        dve.wait_ge(exp_ready, base_u + u + 1)
                        if base_u + u >= 2:
                            dve.wait_ge(p_ready, base_u + u - 1)
                        dve.reciprocal(rinv[:, i:i + 1], rsum[:, i:i + 1]).then_inc(rinv_ready, 1)
                    if s < len(units):
                        lo, hi = keys_of(units[s][2])
                        i = s % 2
                        dve.wait_ge(sc_ready, base_u + s + 1)
                        chain(dve.tensor_reduce(rowmax[:, i:i + 1], sc_bank[i][:, 0:hi - lo], AX.X, ALU.max))
                        dve.tensor_scalar(negmax[:, i:i + 1], rowmax[:, i:i + 1], -SCALE, None,
                                          ALU.mult).then_inc(negmax_ready, 1)
                    if s >= 4:
                        u = s - 4
                        j, h, t = units[u]
                        dve.wait_ge(x_hi, n.next(x_hi))
                        rows = slice(64 * h, 64 * h + 64)
                        dve.tensor_tensor(ol[rows, j, t * P:(t + 1) * P], o_bank[u % 2][rows, 0:P],
                                          oh[rows, j, t * P:(t + 1) * P].bitcast(F32),
                                          ALU.subtract).then_inc(o_ready, 1)
                    taps(TAPS_UNIT[L])
                for i in range(4):
                    rest_to(CHUNK[("gv", L, i)] + 2)
                    taps(TAPS_GV)

                def centre(x):
                    chain(dve.tensor_scalar(rstd[:, 0:nq], STAT[:, 0:nq], 1.0 / CONV, None, ALU.mult))
                    for i in range(4):
                        dve.tensor_tensor(x[:, i, 0:nq], x[:, i, 0:nq], rstd[:, 0:nq], ALU.subtract).then_inc(sub_ready, 1)
                    dve.wait_ge(sub_ready, n.next(sub_ready, 4))

                rest_to(CHUNK[("gu", L, 0)] + 2)
                taps(TAPS_GV)
                dve.wait_ge(mean_psum, 2 * L + 1)
                centre(vT)
                rest_to(CHUNK[("gu", L, 1)] + 2)
                taps(TAPS_GV)
                invert(nq)
                for i in range(4):
                    dve.tensor_tensor(vT[:, i, 0:nq], vT[:, i, 0:nq], rstd[:, 0:nq], ALU.mult).then_inc(norm_t, 1)
                rest_to(CHUNK[("gu", L, 2)] + 2)
                taps(TAPS_GV)
                rest_to(CHUNK[("gu", L, 3)] + 2)
                taps(4 * TAPS)
                dve.wait_ge(mean_psum, 2 * L + 2)
                centre(cacc)
                dve.wait_ge(layer_landed, 16 * 2 * (L + 1))
                for i in range(4):
                    dve.wait_ge(sp_psum, 4 * L + i + 1)
                    nch = nq // P
                    chain(dve.tensor_tensor(
                        msum[:, i % 2, 0:nq].rearrange("p (c t) -> p c t", c=nch),
                        sc_bank[i % 2][:, 0:nq].rearrange("p (c t) -> p c t", c=nch),
                        bsp[:, i:i + 1, :].broadcast_to([P, nch, P]), ALU.add))
                    dve.tensor_tensor(uT[:, i, 0:nq], uT[:, i, 0:nq], msum[:, i % 2, 0:nq], ALU.mult).then_inc(sp_done, 1)
                    dve.wait_ge(sp_done, 4 * L + i + 1)
                    lo_of(gml[:, i, 0:nq], uT[:, i, 0:nq], gmh[:, i, 0:nq])
                rest_to(CHUNK[("gate", L, 0, 0)] + 2)
                invert(nq)
                for i in range(4):
                    dve.tensor_tensor(cacc[:, i, 0:nq], cacc[:, i, 0:nq], rstd[:, 0:nq], ALU.mult).then_inc(norm_t, 1)
                rest_to(CHUNK[("gate", L, 0, 1)] + 2)
                for i in range(4):
                    lo_of(ucl[:, i, 0:nq], vT[:, i, 0:nq], uch[:, i, 0:nq])
                for f in range(8):
                    for b_ in range(3):
                        rest_to(CHUNK[("gate", L, f, b_)] + 2)
                    m0, m1 = msum[:, f % 2, 0:nq], gsig[:, 1, 0:nq]
                    for b_ in range(3):
                        key = ("br", L, f, b_)
                        b, free = (await_part(key, ("br", L, f)) if b_ == 0 else
                                   await_acc(key, (("br", L, f) if b_ == 1 else ("brg", L, f))))
                        if b_ == 0:
                            for gb in range(3):
                                taken(dve, ("gate", L, f, gb))
                            dve.tensor_tensor(m0, b[:, 0:nq], gsig[:, 0, 0:nq], ALU.mult).then_inc(free, 1)
                        else:
                            dve.tensor_tensor(gsig[:, b_, 0:nq], b[:, 0:nq], gsig[:, b_, 0:nq],
                                              ALU.mult).then_inc(free, 1)
                        dve.wait_ge(free, ACC[key] // 2 + 1)
                    chain(dve.tensor_tensor(m0, m0, gsig[:, 1, 0:nq], ALU.add))
                    dve.tensor_tensor(m0, m0, gsig[:, 2, 0:nq], ALU.add).then_inc(norm_t, 1)
                    lo_of(ml[:, f, 0:nq], m0, mh[:, f, 0:nq])
                for f in range(8):
                    rest_to(CHUNK[("out", L, f)] + 2)
                    if L == 0 and f == 0:
                        modulation(L, 16, 48)
                invert(nq)
                residual(0, nq, y16)
                invert(nq)
                if L == 0:
                    modulated(1, TOK, ah, al)
                    k0 = 0
                    for g, ng in enumerate(FF_GROUPS):
                        for i in range(ng):
                            k = k0 + i
                            rest_to(CHUNK[("fa", k)] + 2)
                            b, free = await_acc(("fg", k))
                            taken(dve, ("fa", k))
                            dve.tensor_tensor(fh[:, k % 2, :], b[:], fsil[:, k % 2, :], ALU.mult).then_inc(free, 1)
                            taken(dve, ("fg", k))
                            lo_of(hl[:, i, :], fh[:, k % 2, :], hh[:, i, :])
                        for f in range(8):
                            b, free = await_acc(("f2", g, f))
                            if g == 0:
                                dve.tensor_copy(y16[:, f, :], b[:]).then_inc(free, 1)
                            else:
                                dve.tensor_tensor(y16[:, f, :], b[:], y16[:, f, :], ALU.add).then_inc(free, 1)
                        taken(dve, ("f2", g, 7))
                        k0 += ng
                    invert(TOK)
                    residual(1, TOK, y16)
                else:
                    modulated(1, LAT, None, None)
            dve.wait_ge(const_landed, 16 * (n_const + 3))
            dve.wait_ge(lg_ready, 1)
            for t in range(2):
                chain(dve.max(top[:, t, :], lg[:, t, :]))
                chain(dve.max_index(topi[:, t, :], top[:, t, :], lg[:, t, :]))
                chain(dve.tensor_copy(topf[:, t, :], topi[:, t, :]))
                chain(dve.tensor_scalar(oh1[:, t, :], iota[:, 0:8], topf[:, t, 0:1], None, ALU.is_equal))
                chain(dve.tensor_scalar(oh2[:, t, :], iota[:, 0:8], topf[:, t, 1:2], None, ALU.is_equal))
                ins = dve.tensor_tensor(mask[:, t, :], oh1[:, t, :], oh2[:, t, :], ALU.add)
                if t == 0:
                    chain(ins)
                else:
                    ins.then_inc(mask_ready, 1)
                    dve.wait_ge(mask_ready, 1)
            dve.wait_ge(rank_psum, 1)
            for r in range(2):
                chain(dve.tensor_copy(eid16[:, 8 * r:8 * r + 8], iota[:, 0:8]))
                chain(dve.tensor_scalar(valid[:, 8 * r:8 * r + 8], STAT[:, 16:24], float(SLOTS * r), None,
                                        ALU.is_gt))
            chain(dve.tensor_copy(before[0][:], valid[:]))
            for i, d in enumerate((1, 2, 4, 8)):
                x, y = before[i % 2], before[1 - i % 2]
                chain(dve.tensor_copy(y[:, 0:d], x[:, 0:d]))
                chain(dve.tensor_tensor(y[:, d:16], x[:, d:16], x[:, 0:16 - d], ALU.add))
            chain(dve.tensor_tensor(before[1][:], before[0][:], valid[:], ALU.subtract))

            def per_block(x):
                return x.rearrange("p (o c) -> p o c", o=1).broadcast_to([P, BLOCKS, 16])

            def of_blocks(dst, src):
                chain(dve.tensor_tensor(prod[:], choose[:], per_block(src), ALU.mult))
                chain(dve.tensor_reduce(dst, prod[:], AX.X, ALU.add))

            chain(dve.tensor_tensor(choose[:], per_block(before[1][:]),
                                    iota[:, 0:BLOCKS].rearrange("p (b o) -> p b o", o=1).broadcast_to([P, BLOCKS, 16]),
                                    ALU.is_equal))
            chain(dve.tensor_tensor(choose[:], choose[:], per_block(valid[:]), ALU.mult))
            of_blocks(ids_f[:], eid16[:])
            chain(dve.tensor_copy(ids_i[:], ids_f[:]))
            dve.wait_ge(ft_ready, 4)
            dve.tensor_copy(niter_i[:], before[0][:, 15:16]).then_inc(niter_ready, 1)
            dve.wait_ge(niter_ready, 1)
            for t in range(2):
                chain(dve.scalar_tensor_tensor(rr[:, t, :], STAT[:, 8 * t:8 * t + 8], 1.0, mask[:, t, :],
                                               ALU.add, ALU.mult))
                for r in range(2):
                    chain(dve.tensor_scalar(rr16[:, t, 8 * r:8 * r + 8], rr[:, t, :], -1.0 - SLOTS * r, None,
                                            ALU.add))
                of_blocks(rrp[:, t, :], rr16[:, t, :])
            n_iter = dve.value_load(niter_i[0:1, 0:1], min_val=BLOCKS_MIN, max_val=BLOCKS_MAX)

            def slots_of(col):
                dve.tensor_scalar(S[:, 0, :], iota[:], rrp[:, 0, col], None, ALU.is_equal)
                dve.tensor_scalar(S[:, 1, :], iota[:], rrp[:, 1, col], None, ALU.is_equal).then_inc(s_ready, 1)

            def rest_e(it, c):
                dve.wait_ge(e_hi, it * EN + (c + 1))
                dve.tensor_tensor(elo[c % ESPLIT][:], eraw[c % ERAW][:], ehi[c % ESPLIT][:].bitcast(F32),
                                  ALU.subtract).then_inc(e_lo, 1)

            def rest_gathered(k):
                for half in range(2):
                    dve.wait_ge(xg_hi, k + (half + 1))
                    dve.tensor_tensor(xgl[:, 4 * half:4 * half + 4, :],
                                      ps[6 + half][:].rearrange("p (k s) -> p k s", k=4),
                                      xgh[:, 4 * half:4 * half + 4, :].bitcast(F32), ALU.subtract).then_inc(xg_lo, 1)

            def hidden(it, c, q, half):
                dve.wait_ge(e_used, it * EN + (c + 2))
                dve.wait_ge(silu_done, it * 8 + (2 * q + half + 1))
                dve.tensor_tensor(hq[:, q % 2, half * HN:(half + 1) * HN], acc_bank[1][:, 0:HN], sact[:],
                                  ALU.mult).then_inc(h_done, 1)

            slots_of(slice(0, 1))
            chain(dve.tensor_tensor(ew[:, 0:1], top[:, 0, 1:2], top[:, 0, 0:1], ALU.subtract))
            dve.tensor_tensor(ew[:, 1:2], top[:, 1, 1:2], top[:, 1, 0:1], ALU.subtract).then_inc(e_exp, 1)
            dve.wait_ge(e_exp, 2)
            chain(dve.tensor_scalar(ew[:, 4:6], ew[:, 2:4], 1.0, None, ALU.add))
            chain(dve.reciprocal(ew[:, 6:8], ew[:, 4:6]))
            chain(dve.tensor_tensor(ew[:, 4:6], ew[:, 2:4], ew[:, 6:8], ALU.mult))
            for t in range(2):
                chain(dve.tensor_scalar(oh1[:, t, :], oh1[:, t, :], ew[:, 6 + t:7 + t], None, ALU.mult))
                for r in range(2):
                    chain(dve.scalar_tensor_tensor(wt16[:, t, 8 * r:8 * r + 8], oh2[:, t, :], ew[:, 4 + t:5 + t],
                                                   oh1[:, t, :], ALU.mult, ALU.add))
            for t in range(2):
                of_blocks(wtp[:, t, :], wt16[:, t, :])
            chain(dve.memset(macc[:], 0.0))
            for c in range(ESPLIT):
                rest_e(0, c)
            rest_gathered(0)
            for c in range(ESPLIT, ESPLIT + EPRE - 1):
                rest_e(0, c)
            hidden(0, 2, 0, 0)
            rest_e(0, ESPLIT + EPRE - 1)
            with dve.Fori(0, n_iter) as it:
                c = EPRE
                for kind, q, half in STEPS:
                    if kind == "gather":
                        continue
                    if kind == "turn":
                        dve.wait_ge(hT_hi, it * 4 + (q + 1))
                        dve.tensor_tensor(hTl[:, 0:4, :], ps[4][:].rearrange("p (k s) -> p k s", s=P),
                                          hTh[:, 0:4, :].bitcast(F32), ALU.subtract)
                        dve.tensor_tensor(hTl[:, 4:KQ, :], ps[5][:, 0:3 * P].rearrange("p (k s) -> p k s", s=P),
                                          hTh[:, 4:KQ, :].bitcast(F32), ALU.subtract).then_inc(hT_lo, 1)
                        continue
                    late = (kind, q, half) == ("g", QUARTERS - 1, 1) or (kind, q) == ("w2", QUARTERS - 1)
                    if not late:
                        rest_e(it, c + ESPLIT)
                    if kind == "g":
                        hidden(it, c, q, half)
                    if (kind, q, half) == ("g", QUARTERS - 1, 1):
                        rest_gathered(it * 2 + 2)
                    if (kind, q, half) == ("a", 1, 1):
                        dve.wait_ge(st_ready, it + 1)
                        slots_of(bass.ds(it + 1, 1))
                    if (kind, q) == ("w2", QUARTERS - 1):
                        dve.wait_ge(y_hi, it * 2 + (half + 1))
                        cols = slice(half * 512, half * 512 + 512)
                        dve.tensor_tensor(yl[:, cols], (STAT, MISC)[half][:], yh[:, cols].bitcast(F32),
                                          ALU.subtract).then_inc(y_lo, 1)
                        if half:
                            for m in range(4):
                                t, cols = m % 2, slice(m // 2 * 512, m // 2 * 512 + 512)
                                dve.wait_ge(sct_psum, it * 4 + (m + 1))
                                dve.scalar_tensor_tensor(macc[:, t, cols], ps[4 + t][:], wtp[:, t, bass.ds(it, 1)],
                                                         macc[:, t, cols], ALU.mult, ALU.add).then_inc(sct_done, 1)
                    if late:
                        rest_e(it, c + ESPLIT)
                    rest_e(it, c + ESPLIT + 1)
                    c += 2
            dve.wait_ge(std_ready, n.next(std_ready))
            chain(dve.reciprocal(rcol[:], std[:, 0:2]))
            for t in range(2):
                ins = dve.tensor_scalar(rdiag[:, t, :], ident[:], rcol[:, t:t + 1], None, ALU.mult)
            ins.then_inc(rdiag_ready, 1)
            for k in range(KD):
                dve.wait_ge(mt_psum, k // 2 + 1)
                dve.scalar_tensor_tensor(hres[:, k, 0:LAT], ps[4 + k // 2][:, k % 2 * LAT:(k % 2 + 1) * LAT],
                                         modc[:, 3, 0, k:k + 1], hres[:, k, 0:LAT], ALU.mult, ALU.add
                                         ).then_inc(fin_ready, 1)


COL_Q = 2 * CONV
COL_KV = COL_Q + 384
COL_KR = COL_KV + 256
COL_GM = COL_KR + 32
COL_GATE = COL_GM + 1024
SWAP = [8 * (i // 8 ^ 1) + i % 8 for i in range(32)]


def tiles(w):
    k, n = w.shape[0] // P, w.shape[1]
    w = w.reshape(k, P, n).transpose(1, 0, 2).reshape(P, k * n)
    if k * n < CH:
        w = np.concatenate([w, w[:, :CH - k * n]], axis=1)
    return w


def dense_chunk(a, key):
    kind, L = key[0], key[1]
    w_in = a["w_in"]
    col = {"kv0": COL_KV, "kv1": COL_KV + P, "q0": COL_Q, "q1": COL_Q + P, "q2": COL_Q + 2 * P}
    if kind == "mod":
        _, _, g, kp = key
        return tiles(a["w_mod"][L, kp * 256:(kp + 1) * 256, g * 512:(g + 1) * 512])
    if kind in col:
        return tiles(w_in[L, :, col[kind]:col[kind] + P])
    if kind == "kr":
        kr = w_in[L, :, COL_KR:COL_KR + 32]
        return tiles(np.concatenate([kr, kr, kr, kr[:, SWAP]], axis=1))
    if kind in ("ca", "cg", "gu", "gv"):
        c = {"ca": 0, "cg": CONV, "gu": COL_GM, "gv": COL_GM + CONV}[kind] + key[2] * P
        return tiles(w_in[L, :, c:c + P])
    if kind in ("uk", "uv"):
        w = a["w_ukv"][L].reshape(256, HEADS, 128)
        return tiles((w[:, :, :NOPE] if kind == "uk" else w[:, :, NOPE:]).reshape(256, 512))
    if kind == "uq":
        w = a["w_uq"][L].reshape(384, HEADS, QK_HEAD)[:, 2 * key[2]:2 * key[2] + 2]
        return tiles(np.concatenate([w, w[:, :, NOPE:][:, :, SWAP]], axis=2).reshape(384, 256))
    if kind == "gate":
        c = COL_GATE + key[3] * D + key[2] * P
        return tiles(w_in[L, :, c:c + P])
    if kind == "br":
        c = slice(key[2] * P, key[2] * P + P)
        return tiles(np.concatenate([a["w_conv_out"][L, :, c], a["w_attn_out"][L, :, c]], axis=0))
    if kind == "brg":
        return tiles(a["w_gmlp_out"][L, :, key[2] * P:key[2] * P + P])
    if kind == "out":
        return tiles(a["w_out"][L, :, key[2] * P:key[2] * P + P])
    if kind in ("fa", "fg"):
        c = key[1] * P + (FF if kind == "fg" else 0)
        return tiles(a["ffn_w13"][0, :, c:c + P])
    k0 = sum(FF_GROUPS[:key[1]]) * P
    return tiles(a["ffn_w2"][0, k0:k0 + FF_GROUPS[key[1]] * P, key[2] * P:key[2] * P + P])


def expert_chunks(a):
    w13 = a["moe_w13"][0].reshape(EXPERTS, 2, KD // 2, P, 2, QUARTERS, 2, HN)
    w2 = a["moe_w2"][0].reshape(EXPERTS, QUARTERS, KQ, P, 2, 2, 256)
    out = np.empty((EXPERTS, EN, P, ECH), np.float32)
    for c, (kind, q, half, p) in enumerate(ECHUNKS):
        w = w2[:, q, :, :, half, p] if kind == "w2" else w13[:, p, :, :, "ag".index(kind), q % QUARTERS, half]
        out[:, stored(c)] = w.transpose(0, 2, 1, 3).reshape(EXPERTS, P, ECH)
    return out


def rotations():
    inv = np.float32(10000.0) ** (-np.arange(8, dtype=np.float32) / np.float32(8))
    t = np.arange(LAT)
    row, col = (t // 64).astype(np.float32), (t % 64).astype(np.float32)
    ang = np.concatenate([inv[:, None] * row] * 2 + [inv[:, None] * col] * 2, axis=0)
    sign = np.where(np.arange(32) // 8 % 2 == 0, -1.0, 1.0)[:, None]
    out = np.zeros((P, LAT), np.float32)
    out[64:96] = np.cos(ang)
    out[96:128] = np.sin(ang) * sign
    return out


def kernel(**inputs):
    import concourse.bacc as bacc
    from concourse.bass_utils import run_bass_kernel_spmd

    a = {k: np.asarray(v) for k, v in inputs.items()}
    tok = np.concatenate([a["x"][0], a["ctx"][0]], axis=0)
    arrays = {
        "xT": tok.T.reshape(KD, P, TOK).transpose(1, 0, 2),
        "cvec": np.stack([a["c"][0], a["c_ctx"]], axis=1).reshape(KD, P, 2).transpose(1, 0, 2),
        "par": np.stack([np.concatenate(
            [a[name][L].reshape(TAPS, 4, P).transpose(2, 1, 0).reshape(P, 4 * TAPS) if name == "conv_dw"
             else a[name][L].reshape(-1, P).T for name, _ in PARAMS], axis=1) for L in range(LAYERS)]),
        "ident": np.eye(P, dtype=np.float32),
        "ones": np.ones((P, P), np.float32),
        "upper": np.triu(np.ones((P, P), np.float32), 1),
        "iota": np.tile(np.arange(SLOTS, dtype=np.float32), (P, 1)),
        "sel2": np.tile(np.eye(2, dtype=np.float32), (2, 1)),
        "rope": rotations(),
        "wsT": a["w_spatial"].transpose(0, 3, 1, 2),
        "bsp": np.repeat(a["b_spatial"].reshape(LAYERS, 4, 2, 1, P), 64, axis=3).reshape(
            LAYERS, 4, P, P).transpose(0, 2, 1, 3),
        "rw": a["router_w"][0].reshape(KD, P, EXPERTS).transpose(1, 0, 2),
        "dense": np.stack([dense_chunk(a, key) for key in CHUNK]),
        "moe": expert_chunks(a),
    }
    arrays = {k: np.ascontiguousarray(v) for k, v in arrays.items()}
    nc = bacc.Bacc("TRN2", target_bir_lowering=False, num_devices=1)
    A = {k: nc.dram_tensor(f"in_{k}", v.shape, F32, kind="ExternalInput").ap() for k, v in arrays.items()}
    out = nc.dram_tensor("out_h", (P, KD, LAT), F32, kind="ExternalOutput").ap()
    build(nc, A, out)
    r = run_bass_kernel_spmd(nc, [{f"in_{k}": v for k, v in arrays.items()}], core_ids=[0])
    return r.results[0]["out_h"].transpose(2, 1, 0).reshape(1, LAT, D)
```
